# Optimizing a Trainium2 kernel written in Bass

```python
import numpy as np
import jax
import jax.numpy as jnp
from jax import lax
import math

D_MODEL = 1024
BATCH = 1
SEQ = 256
DEPTH = 2

HEAD_DIM = 64
ROT_DIM = HEAD_DIM // 4
ROPE_THETA = 500000.0
NORM_EPS = 1e-6
Q_BLOCK = 128
D_FF = 2816
NEG_INF = -1e30

A_GROUPS = 4
A_CHUNK = 128
A_WIDTH = A_GROUPS * HEAD_DIM
B_HEADS = 12
B_KV_HEADS = 3
B_WIDTH = B_HEADS * HEAD_DIM
B_KV_WIDTH = B_KV_HEADS * HEAD_DIM
CMP_LEN = 32
CMP_STRIDE = 16
CMP_HIDDEN = 256
SLC_BLOCK = 64
SLC_TOPN = 8
WINDOW = 512
N_BRANCH = 3
FORCE_SCORE = 1e4
C_HEADS = 8
C_WIDTH = C_HEADS * HEAD_DIM
IDX_HEADS = 4
IDX_DIM = 32
IDX_ROT = IDX_DIM // 4
DSA_TOPK = 256
D_HEADS = 8
D_WIDTH = D_HEADS * HEAD_DIM
MOBA_BLOCK = 256
MOBA_TOPK = 3

EVEN_SPLITS = (2 * A_WIDTH, B_WIDTH) + (B_KV_WIDTH,) * 6 + (B_HEADS * N_BRANCH,)
ODD_SPLITS = (C_WIDTH, HEAD_DIM, HEAD_DIM, IDX_HEADS * IDX_DIM, IDX_DIM, IDX_HEADS, D_WIDTH, D_WIDTH, D_WIDTH)
EVEN_IN = sum(EVEN_SPLITS)
ODD_IN = sum(ODD_SPLITS)
MIX_OUT = A_WIDTH + B_WIDTH
N_EVEN = (DEPTH + 1) // 2
N_ODD = DEPTH // 2


def rmsnorm(x, g):
    xf = x.astype(jnp.float32)
    y = xf * lax.rsqrt(jnp.mean(xf * xf, axis=-1, keepdims=True) + NORM_EPS)
    return (y * g.astype(jnp.float32)).astype(x.dtype)

def rope_tables(positions, rot_dim):
    inv_freq = ROPE_THETA ** (-jnp.arange(0, rot_dim, 2, dtype=jnp.float32) / rot_dim)
    ang = positions.astype(jnp.float32)[..., None] * inv_freq
    return jnp.cos(ang), jnp.sin(ang)

def partial_rope(x, cos, sin):
    half = cos.shape[-1]
    bshape = cos.shape[:2] + (1,) * (x.ndim - 3) + (half,)
    c = cos.reshape(bshape).astype(x.dtype)
    s = sin.reshape(bshape).astype(x.dtype)
    x1, x2, rest = x[..., :half], x[..., half:2 * half], x[..., 2 * half:]
    return jnp.concatenate([x1 * c - x2 * s, x2 * c + x1 * s, rest], axis=-1)

def masked_softmax(s, mask):
    s = jnp.where(mask, s.astype(jnp.float32), NEG_INF)
    return jnp.where(mask, jax.nn.softmax(s, axis=-1), 0.0)

def swiglu_ffn(x, g, w_gate, w_up, w_down):
    h = rmsnorm(x, g)
    return (jax.nn.silu(h @ w_gate) * (h @ w_up)) @ w_down

def split_cols(z, sizes):
    return jnp.split(z, [int(c) for c in np.cumsum(sizes)[:-1]], axis=-1)

def rows(a, b, q0):
    return lax.dynamic_slice_in_dim(a[b], q0, Q_BLOCK, axis=0)

def map_query_blocks(fn, batch, seq):
    n_qb = seq // Q_BLOCK

    def step(i):
        return fn(i // n_qb, (i % n_qb) * Q_BLOCK)

    out = lax.map(step, jnp.arange(batch * n_qb, dtype=jnp.int32))
    return out.reshape((batch, seq) + out.shape[2:])

def chunked_gmlp(z, sgu_norm, sgu_w, sgu_b):
    bsz, seq, _ = z.shape
    u, v = jnp.split(jax.nn.gelu(z), 2, axis=-1)
    v = rmsnorm(v, sgu_norm).reshape(bsz, seq // A_CHUNK, A_CHUNK, A_GROUPS, HEAD_DIM)
    causal = jnp.tril(jnp.ones((A_CHUNK, A_CHUNK), dtype=bool))
    w = jnp.where(causal, sgu_w, jnp.zeros_like(sgu_w))
    mixed = jnp.einsum('gts,bcsgd->bctgd', w, v) + sgu_b.T[:, :, None]
    return u * mixed.reshape(bsz, seq, A_WIDTH)

def compress_blocks(t, pos_emb, w1, w2):
    bsz, seq = t.shape[:2]
    n_cmp = (seq - CMP_LEN) // CMP_STRIDE + 1
    idx = jnp.arange(n_cmp)[:, None] * CMP_STRIDE + jnp.arange(CMP_LEN)[None, :]
    blk = t[:, idx] + pos_emb[:, None, :]
    blk = jnp.moveaxis(blk, 3, 2).reshape(bsz, n_cmp, B_KV_HEADS, CMP_LEN * HEAD_DIM)
    return jax.nn.gelu(blk @ w1) @ w2

def cmp_to_slc_overlap(n_cmp, n_slc):
    c0 = np.arange(n_cmp) * CMP_STRIDE
    s0 = np.arange(n_slc) * SLC_BLOCK
    m = (c0[:, None] < s0[None, :] + SLC_BLOCK) & (c0[:, None] + CMP_LEN > s0[None, :])
    return jnp.asarray(m, dtype=jnp.float32)

def nsa_attention(q_rot, q_raw, k_cmp, v_cmp, k_slc, v_slc, k_win, v_win, gates):
    bsz, seq = q_rot.shape[:2]
    grp = B_HEADS // B_KV_HEADS
    scale = HEAD_DIM ** -0.5
    n_cmp = k_cmp.shape[1]
    n_slc = seq // SLC_BLOCK
    top_n = min(SLC_TOPN, n_slc)
    overlap = cmp_to_slc_overlap(n_cmp, n_slc)
    cmp_end = jnp.arange(n_cmp) * CMP_STRIDE + CMP_LEN - 1
    blk_id = jnp.arange(n_slc)
    k_blk = k_slc.reshape(bsz, n_slc, SLC_BLOCK, B_KV_HEADS, HEAD_DIM).transpose(0, 3, 1, 2, 4)
    v_blk = v_slc.reshape(bsz, n_slc, SLC_BLOCK, B_KV_HEADS, HEAD_DIM).transpose(0, 3, 1, 2, 4)
    pad = jnp.zeros((bsz, WINDOW, B_KV_HEADS, HEAD_DIM), k_win.dtype)
    k_win_p = jnp.concatenate([pad, k_win], axis=1)
    v_win_p = jnp.concatenate([pad, v_win], axis=1)
    g_idx = jnp.arange(B_KV_HEADS)[:, None, None]
    win_off = jnp.arange(Q_BLOCK + WINDOW) - WINDOW

    def block(b, q0):
        t = q0 + jnp.arange(Q_BLOCK)
        qr = rows(q_rot, b, q0).reshape(Q_BLOCK, B_KV_HEADS, grp, HEAD_DIM)
        qn = rows(q_raw, b, q0).reshape(Q_BLOCK, B_KV_HEADS, grp, HEAD_DIM)
        s_c = jnp.einsum('qgrd,ngd->grqn', qn, k_cmp[b]) * scale
        p_c = masked_softmax(s_c, cmp_end[None, :] <= t[:, None])
        o_c = jnp.einsum('grqn,ngd->qgrd', p_c.astype(v_cmp.dtype), v_cmp[b])
        imp = jnp.einsum('grqn,nj->gqj', p_c, overlap)
        admissible = blk_id[None, :] * SLC_BLOCK <= t[:, None]
        forced = (blk_id[None, :] == 0) | (blk_id[None, :] == t[:, None] // SLC_BLOCK)
        imp = jnp.where(admissible, jnp.where(forced, FORCE_SCORE, imp), NEG_INF)
        _, sel = lax.top_k(imp, top_n)
        sel_ok = jnp.take_along_axis(jnp.broadcast_to(admissible, imp.shape), sel, axis=-1)
        ks = k_blk[b][g_idx, sel].reshape(B_KV_HEADS, Q_BLOCK, top_n * SLC_BLOCK, HEAD_DIM)
        vs = v_blk[b][g_idx, sel].reshape(B_KV_HEADS, Q_BLOCK, top_n * SLC_BLOCK, HEAD_DIM)
        tok = (sel[..., None] * SLC_BLOCK + jnp.arange(SLC_BLOCK)).reshape(B_KV_HEADS, Q_BLOCK, top_n * SLC_BLOCK)
        m_s = (tok <= t[None, :, None]) & jnp.repeat(sel_ok, SLC_BLOCK, axis=-1)
        s_s = jnp.einsum('qgrd,gqkd->grqk', qr, ks) * scale
        p_s = masked_softmax(s_s, m_s[:, None])
        o_s = jnp.einsum('grqk,gqkd->qgrd', p_s.astype(vs.dtype), vs)
        kw = lax.dynamic_slice_in_dim(k_win_p[b], q0, Q_BLOCK + WINDOW, axis=0)
        vw = lax.dynamic_slice_in_dim(v_win_p[b], q0, Q_BLOCK + WINDOW, axis=0)
        s_pos = q0 + win_off
        m_w = (s_pos[None, :] <= t[:, None]) & (s_pos[None, :] > t[:, None] - WINDOW) & (s_pos[None, :] >= 0)
        s_w = jnp.einsum('qgrd,kgd->grqk', qr, kw) * scale
        p_w = masked_softmax(s_w, m_w)
        o_w = jnp.einsum('grqk,kgd->qgrd', p_w.astype(vw.dtype), vw)
        g = rows(gates, b, q0).reshape(Q_BLOCK, B_KV_HEADS, grp, N_BRANCH)
        o = g[..., 0:1] * o_c + g[..., 1:2] * o_s + g[..., 2:3] * o_w
        return o.reshape(Q_BLOCK, B_WIDTH)

    return map_query_blocks(block, bsz, seq)

def dsa_attention(q, k, v, q_idx, k_idx, w_idx):
    bsz, seq = q.shape[:2]
    top_k = min(DSA_TOPK, seq // 4)
    scale = HEAD_DIM ** -0.5
    key_pos = jnp.arange(seq)

    def block(b, q0):
        t = q0 + jnp.arange(Q_BLOCK)
        qb = rows(q, b, q0)
        logits = jnp.einsum('qhd,sd->qhs', rows(q_idx, b, q0), k_idx[b]).astype(jnp.float32) * IDX_DIM ** -0.5
        score = jnp.einsum('qh,qhs->qs', rows(w_idx, b, q0).astype(jnp.float32), jax.nn.relu(logits)) * IDX_HEADS ** -0.5
        score = jnp.where(key_pos[None, :] <= t[:, None], score, NEG_INF)
        _, sel = lax.top_k(score, top_k)
        ok = sel <= t[:, None]
        ks = k[b][sel]
        vs = v[b][sel]
        s = jnp.einsum('qhd,qkd->hqk', qb, ks) * scale
        p = masked_softmax(s, ok[None])
        o = jnp.einsum('hqk,qkd->qhd', p.astype(vs.dtype), vs)
        return o.reshape(Q_BLOCK, C_WIDTH)

    return map_query_blocks(block, bsz, seq)

def moba_attention(q, k, v):
    bsz, seq = q.shape[:2]
    n_blk = -(-seq // MOBA_BLOCK)
    pad = n_blk * MOBA_BLOCK - seq
    scale = HEAD_DIM ** -0.5
    k_blk = jnp.pad(k, ((0, 0), (0, pad), (0, 0), (0, 0))).reshape(bsz, n_blk, MOBA_BLOCK, D_HEADS, HEAD_DIM).transpose(0, 3, 1, 2, 4)
    v_blk = jnp.pad(v, ((0, 0), (0, pad), (0, 0), (0, 0))).reshape(bsz, n_blk, MOBA_BLOCK, D_HEADS, HEAD_DIM).transpose(0, 3, 1, 2, 4)
    k_mean = k_blk.mean(axis=3)
    top_k = min(MOBA_TOPK, n_blk - 1)
    blk_id = jnp.arange(n_blk)
    h_idx = jnp.arange(D_HEADS)[:, None, None]

    def block(b, q0):
        t = q0 + jnp.arange(Q_BLOCK)
        qb = rows(q, b, q0)
        own = q0 // MOBA_BLOCK
        k_own = lax.dynamic_index_in_dim(k_blk[b], own, axis=1, keepdims=False)
        v_own = lax.dynamic_index_in_dim(v_blk[b], own, axis=1, keepdims=False)
        own_pos = own * MOBA_BLOCK + jnp.arange(MOBA_BLOCK)
        s_own = jnp.einsum('qhd,hkd->hqk', qb, k_own) * scale
        m_own = jnp.broadcast_to(own_pos[None, :] <= t[:, None], s_own.shape)
        if top_k == 0:
            p = masked_softmax(s_own, m_own)
            o = jnp.einsum('hqk,hkd->qhd', p.astype(v_own.dtype), v_own)
        else:
            gate = jnp.einsum('qhd,hjd->hqj', qb, k_mean[b]).astype(jnp.float32)
            gate = jnp.where(blk_id < own, gate, NEG_INF)
            _, sel = lax.top_k(gate, top_k)
            ok = sel < own
            n_sel = top_k * MOBA_BLOCK
            ks = k_blk[b][h_idx, sel].reshape(D_HEADS, Q_BLOCK, n_sel, HEAD_DIM)
            vs = v_blk[b][h_idx, sel].reshape(D_HEADS, Q_BLOCK, n_sel, HEAD_DIM)
            s_sel = jnp.einsum('qhd,hqkd->hqk', qb, ks) * scale
            m_sel = jnp.repeat(ok, MOBA_BLOCK, axis=-1)
            p = masked_softmax(jnp.concatenate([s_sel, s_own], axis=-1), jnp.concatenate([m_sel, m_own], axis=-1))
            o = (jnp.einsum('hqk,hqkd->qhd', p[..., :n_sel].astype(vs.dtype), vs)
                 + jnp.einsum('hqk,hkd->qhd', p[..., n_sel:].astype(v_own.dtype), v_own))
        return o.reshape(Q_BLOCK, D_WIDTH)

    return map_query_blocks(block, bsz, seq)

def even_mixer(h, cos, sin, w_in, sgu_norm, sgu_w, sgu_b, cmp_pos_k, cmp_w1_k, cmp_w2_k,
               cmp_pos_v, cmp_w1_v, cmp_w2_v, w_out):
    bsz, seq, _ = h.shape
    a_in, q, kc, vc, ksl, vsl, kw, vw, gl = split_cols(h @ w_in, EVEN_SPLITS)

    def kv(t):
        return t.reshape(bsz, seq, B_KV_HEADS, HEAD_DIM)

    q_raw = q.reshape(bsz, seq, B_HEADS, HEAD_DIM)
    a_out = chunked_gmlp(a_in, sgu_norm, sgu_w, sgu_b)
    b_out = nsa_attention(partial_rope(q_raw, cos, sin), q_raw,
                          compress_blocks(kv(kc), cmp_pos_k, cmp_w1_k, cmp_w2_k),
                          compress_blocks(kv(vc), cmp_pos_v, cmp_w1_v, cmp_w2_v),
                          partial_rope(kv(ksl), cos, sin), kv(vsl),
                          partial_rope(kv(kw), cos, sin), kv(vw),
                          jax.nn.sigmoid(gl).reshape(bsz, seq, B_HEADS, N_BRANCH))
    return jnp.concatenate([a_out, b_out], axis=-1) @ w_out

def odd_mixer(h, cos, sin, cos_i, sin_i, w_in, w_out):
    bsz, seq, _ = h.shape
    qc, kc, vc, qi, ki, wi, qd, kd, vd = split_cols(h @ w_in, ODD_SPLITS)
    c_out = dsa_attention(partial_rope(qc.reshape(bsz, seq, C_HEADS, HEAD_DIM), cos, sin),
                          partial_rope(kc, cos, sin), vc,
                          partial_rope(qi.reshape(bsz, seq, IDX_HEADS, IDX_DIM), cos_i, sin_i),
                          partial_rope(ki, cos_i, sin_i), wi)
    d_out = moba_attention(partial_rope(qd.reshape(bsz, seq, D_HEADS, HEAD_DIM), cos, sin),
                           partial_rope(kd.reshape(bsz, seq, D_HEADS, HEAD_DIM), cos, sin),
                           vd.reshape(bsz, seq, D_HEADS, HEAD_DIM))
    return jnp.concatenate([c_out, d_out], axis=-1) @ w_out

def first_inputs(seed: int = 0) -> dict:
    key = jax.random.key(seed)
    keys = iter(jax.random.split(key, 40))

    def nrm(shape, scale):
        return jax.random.normal(next(keys), shape, jnp.float32) * scale

    def gain(shape):
        return 1.0 + nrm(shape, 0.1)

    x = nrm((BATCH, SEQ, D_MODEL), 1.0)
    offset = jax.random.randint(next(keys), (BATCH, 1), 0, 4096, dtype=jnp.int32)
    positions = offset + jnp.arange(SEQ, dtype=jnp.int32)[None, :]
    return {
        'x': x,
        'positions': positions,
        'ffn1_norm': gain((DEPTH, D_MODEL)),
        'ffn1_w_gate': nrm((DEPTH, D_MODEL, D_FF), D_MODEL ** -0.5),
        'ffn1_w_up': nrm((DEPTH, D_MODEL, D_FF), D_MODEL ** -0.5),
        'ffn1_w_down': nrm((DEPTH, D_FF, D_MODEL), D_FF ** -0.5),
        'mix_norm': gain((DEPTH, D_MODEL)),
        'ffn2_norm': gain((DEPTH, D_MODEL)),
        'ffn2_w_gate': nrm((DEPTH, D_MODEL, D_FF), D_MODEL ** -0.5),
        'ffn2_w_up': nrm((DEPTH, D_MODEL, D_FF), D_MODEL ** -0.5),
        'ffn2_w_down': nrm((DEPTH, D_FF, D_MODEL), D_FF ** -0.5),
        'ev_w_in': nrm((N_EVEN, D_MODEL, EVEN_IN), D_MODEL ** -0.5),
        'ev_sgu_norm': gain((N_EVEN, A_WIDTH)),
        'ev_sgu_w': nrm((N_EVEN, A_GROUPS, A_CHUNK, A_CHUNK), A_CHUNK ** -0.5),
        'ev_sgu_b': gain((N_EVEN, A_GROUPS, A_CHUNK)),
        'ev_cmp_pos_k': nrm((N_EVEN, CMP_LEN, HEAD_DIM), 0.1),
        'ev_cmp_w1_k': nrm((N_EVEN, CMP_LEN * HEAD_DIM, CMP_HIDDEN), (CMP_LEN * HEAD_DIM) ** -0.5),
        'ev_cmp_w2_k': nrm((N_EVEN, CMP_HIDDEN, HEAD_DIM), CMP_HIDDEN ** -0.5),
        'ev_cmp_pos_v': nrm((N_EVEN, CMP_LEN, HEAD_DIM), 0.1),
        'ev_cmp_w1_v': nrm((N_EVEN, CMP_LEN * HEAD_DIM, CMP_HIDDEN), (CMP_LEN * HEAD_DIM) ** -0.5),
        'ev_cmp_w2_v': nrm((N_EVEN, CMP_HIDDEN, HEAD_DIM), CMP_HIDDEN ** -0.5),
        'ev_w_out': nrm((N_EVEN, MIX_OUT, D_MODEL), MIX_OUT ** -0.5),
        'od_w_in': nrm((N_ODD, D_MODEL, ODD_IN), D_MODEL ** -0.5),
        'od_w_out': nrm((N_ODD, MIX_OUT, D_MODEL), MIX_OUT ** -0.5),
        'final_norm': gain((D_MODEL,)),
    }

def first_block(x, positions, ffn1_norm, ffn1_w_gate, ffn1_w_up, ffn1_w_down, mix_norm,
              ffn2_norm, ffn2_w_gate, ffn2_w_up, ffn2_w_down, ev_w_in, ev_sgu_norm, ev_sgu_w,
              ev_sgu_b, ev_cmp_pos_k, ev_cmp_w1_k, ev_cmp_w2_k, ev_cmp_pos_v, ev_cmp_w1_v,
              ev_cmp_w2_v, ev_w_out, od_w_in, od_w_out, final_norm):
    cos, sin = rope_tables(positions, ROT_DIM)
    cos_i, sin_i = rope_tables(positions, IDX_ROT)
    for i in range(DEPTH):
        x = x + 0.5 * swiglu_ffn(x, ffn1_norm[i], ffn1_w_gate[i], ffn1_w_up[i], ffn1_w_down[i])
        h = rmsnorm(x, mix_norm[i])
        if i % 2 == 0:
            e = i // 2
            x = x + even_mixer(h, cos, sin, ev_w_in[e], ev_sgu_norm[e], ev_sgu_w[e], ev_sgu_b[e],
                               ev_cmp_pos_k[e], ev_cmp_w1_k[e], ev_cmp_w2_k[e],
                               ev_cmp_pos_v[e], ev_cmp_w1_v[e], ev_cmp_w2_v[e], ev_w_out[e])
        else:
            o = i // 2
            x = x + odd_mixer(h, cos, sin, cos_i, sin_i, od_w_in[o], od_w_out[o])
        x = x + 0.5 * swiglu_ffn(x, ffn2_norm[i], ffn2_w_gate[i], ffn2_w_up[i], ffn2_w_down[i])
    return rmsnorm(x, final_norm)


RWKV_HEADS = 8
RWKV_HEAD_DIM = 64
RWKV_WIDTH = RWKV_HEADS * RWKV_HEAD_DIM
DECAY_LORA = 64
ICLR_LORA = 64
VRES_LORA = 32
GATE_LORA = 128
RWKV_GN_EPS = 64e-5
MLA_HEADS = 8
QK_NOPE_DIM = 64
QK_ROPE_DIM = 32
MLA_QK_DIM = QK_NOPE_DIM + QK_ROPE_DIM
MLA_V_DIM = 64
MLA_WIDTH = MLA_HEADS * MLA_V_DIM
Q_LORA_RANK = 256
KV_LORA_RANK = 128
ROPE_THETA_2 = 10000.0
GDN_HEADS = 8
GDN_K_DIM = 64
GDN_V_DIM = 64
GDN_WIDTH = GDN_HEADS * GDN_V_DIM
GDN_QKV = 2 * GDN_HEADS * GDN_K_DIM + GDN_HEADS * GDN_V_DIM
GDN_CONV = 4
GDN_CHUNK = 64
FF_DENSE = 2816
N_EXPERTS = 8
TOP_K = 2
FF_EXPERT = 3584
MOE_BLOCK = 128
PLE_DIM = 256

RWKV_IN_SIZES = (RWKV_WIDTH, RWKV_WIDTH, RWKV_WIDTH, DECAY_LORA, ICLR_LORA, GATE_LORA)
MLA_IN_SIZES = (Q_LORA_RANK, KV_LORA_RANK, QK_ROPE_DIM)
GDN_IN_SIZES = (GDN_QKV, GDN_HEADS, GDN_HEADS, GDN_WIDTH)
RWKV_IN = sum(RWKV_IN_SIZES)
MLA_IN = sum(MLA_IN_SIZES)
GDN_IN = sum(GDN_IN_SIZES)
GATE_IN = N_BRANCH * D_MODEL
N_IN = RWKV_IN + MLA_IN + GDN_IN + GATE_IN


def rms_norm(x, g, eps=NORM_EPS):
    xf = x.astype(jnp.float32)
    y = xf * lax.rsqrt(jnp.mean(jnp.square(xf), axis=-1, keepdims=True) + eps)
    return (y * g.astype(jnp.float32)).astype(x.dtype)

def l2_normalize(x, eps=1e-12):
    xf = x.astype(jnp.float32)
    return xf * lax.rsqrt(jnp.sum(jnp.square(xf), axis=-1, keepdims=True) + eps)

def split_cols_2(z, sizes):
    return jnp.split(z, [int(c) for c in np.cumsum(sizes)[:-1]], axis=-1)

def heads(t, n):
    return t.reshape(t.shape[:-1] + (n, t.shape[-1] // n))

def token_shift(z):
    return jnp.pad(z, ((0, 0), (1, 0), (0, 0)))[:, :-1]

def rope_tables_2(positions):
    inv_freq = 1.0 / (ROPE_THETA_2 ** (jnp.arange(0, QK_ROPE_DIM, 2, dtype=jnp.float32) / QK_ROPE_DIM))
    ang = positions.astype(jnp.float32)[..., None] * inv_freq
    return jnp.cos(ang)[:, :, None, :], jnp.sin(ang)[:, :, None, :]

def apply_rope(x, cos, sin):
    x1, x2 = jnp.split(x.astype(jnp.float32), 2, axis=-1)
    return jnp.concatenate([x1 * cos - x2 * sin, x2 * cos + x1 * sin], axis=-1).astype(x.dtype)

def rwkv7_recurrence(r, w, k, v, a, b):
    bsz, _, h, n = r.shape

    def step(state, xs):
        r_t, w_t, k_t, v_t, a_t, b_t = xs
        sa = jnp.einsum('bhij,bhj->bhi', state, a_t)
        state = (state * w_t[:, :, None, :] + sa[..., None] * b_t[:, :, None, :]
                 + v_t[..., None] * k_t[:, :, None, :])
        return state, jnp.einsum('bhij,bhj->bhi', state, r_t)

    xs = tuple(jnp.moveaxis(t, 1, 0) for t in (r, w, k, v, a, b))
    _, y = lax.scan(step, jnp.zeros((bsz, h, n, n), jnp.float32), xs)
    return jnp.moveaxis(y, 0, 1)

def rwkv7_branch(z, u, v_first, vres, mu, w0, w_up, a0, a_up, g_up, k_k, k_a, r_k, ln_g, ln_b):
    b, s, _ = z.shape
    z = z + (token_shift(z) - z) * mu
    r, k, v, w_lo, a_lo, g_lo = split_cols_2(z, RWKV_IN_SIZES)
    log_w = -jax.nn.softplus(-(w0 + jnp.tanh(w_lo) @ w_up)) - 0.5
    decay = jnp.exp(-jnp.exp(log_w.astype(jnp.float32)))
    iclr = jax.nn.sigmoid(a0 + a_lo @ a_up)
    gate = jax.nn.sigmoid(g_lo) @ g_up
    if vres is None:
        v_first = v
    else:
        v_mu, v_down, v_up, v_bias = vres
        xv = u + (token_shift(u) - u) * v_mu
        v = v + (v_first - v) * jax.nn.sigmoid(v_bias + (xv @ v_down) @ v_up)
    kk = l2_normalize(heads(k * k_k, RWKV_HEADS))
    k = k * (1.0 + (iclr - 1.0) * k_a)
    rh, kh, vh, ah, wh = (heads(t, RWKV_HEADS).astype(jnp.float32) for t in (r, k, v, iclr, decay))
    y = rwkv7_recurrence(rh, wh, kh, vh, -kk, kk * ah)
    mean = jnp.mean(y, axis=-1, keepdims=True)
    var = jnp.mean(jnp.square(y - mean), axis=-1, keepdims=True)
    y = ((y - mean) * lax.rsqrt(var + RWKV_GN_EPS)).reshape(b, s, RWKV_WIDTH) * ln_g + ln_b
    bonus = jnp.sum(rh * kh * r_k, axis=-1, keepdims=True) * vh
    y = y + bonus.reshape(b, s, RWKV_WIDTH)
    return (y * gate).astype(z.dtype), v_first

def causal_block_attention(q, k, v, scale):
    seq = q.shape[1]
    outs = []
    for start in range(0, seq, Q_BLOCK):
        stop = start + Q_BLOCK
        s = jnp.einsum('bqhd,bkhd->bhqk', q[:, start:stop], k[:, :stop]).astype(jnp.float32) * scale
        mask = (start + jnp.arange(Q_BLOCK))[:, None] >= jnp.arange(stop)[None, :]
        prob = jax.nn.softmax(jnp.where(mask, s, -jnp.inf), axis=-1)
        outs.append(jnp.einsum('bhqk,bkhd->bqhd', prob.astype(v.dtype), v[:, :stop]))
    return jnp.concatenate(outs, axis=1)

def mla_branch(z, cos, sin, q_norm_g, kv_norm_g, w_uq, w_ukv, qk_g_q, qk_g_k):
    b, s, _ = z.shape
    c_q, c_kv, k_pe = split_cols_2(z, MLA_IN_SIZES)
    q = heads(rms_norm(c_q, q_norm_g) @ w_uq, MLA_HEADS)
    kv = heads(rms_norm(c_kv, kv_norm_g) @ w_ukv, MLA_HEADS)
    k_nope, v = kv[..., :QK_NOPE_DIM], kv[..., QK_NOPE_DIM:]
    k_pe = jnp.broadcast_to(k_pe[:, :, None, :], k_nope.shape[:-1] + (QK_ROPE_DIM,))
    k = jnp.concatenate([k_nope, k_pe], axis=-1)
    q = rms_norm(q, qk_g_q)
    k = rms_norm(k, qk_g_k)
    q = jnp.concatenate([q[..., :QK_NOPE_DIM], apply_rope(q[..., QK_NOPE_DIM:], cos, sin)], axis=-1)
    k = jnp.concatenate([k[..., :QK_NOPE_DIM], apply_rope(k[..., QK_NOPE_DIM:], cos, sin)], axis=-1)
    o = causal_block_attention(q, k, v, MLA_QK_DIM ** -0.5)
    return o.reshape(b, s, MLA_WIDTH)

def causal_depthwise_conv(x, w):
    xp = jnp.pad(x, ((0, 0), (GDN_CONV - 1, 0), (0, 0)))
    return lax.conv_general_dilated(xp, w[:, None, :].astype(x.dtype), (1,), 'VALID',
                                    dimension_numbers=('NWC', 'WIO', 'NWC'),
                                    feature_group_count=x.shape[-1])

def chunk_gated_delta_rule(q, k, v, g, beta):
    b, s, h, dk = q.shape
    dv = v.shape[-1]
    c = GDN_CHUNK
    n = s // c

    def chunks(t):
        return jnp.moveaxis(t.reshape((b, n, c, h) + t.shape[3:]), 3, 2)

    q, k, v, g, beta = (chunks(t) for t in (q, k, v, g, beta))
    gc = jnp.cumsum(g, axis=-1)
    causal = jnp.tril(jnp.ones((c, c), dtype=bool))
    strict = jnp.tril(jnp.ones((c, c), dtype=bool), -1)
    gamma = jnp.exp(jnp.where(causal, gc[..., :, None] - gc[..., None, :], -jnp.inf))
    kb = k * beta[..., None]
    m = jnp.where(strict, jnp.einsum('bnhid,bnhjd->bnhij', kb, k) * gamma, 0.0) + jnp.eye(c, dtype=jnp.float32)
    rhs = jnp.concatenate([v * beta[..., None], kb * jnp.exp(gc)[..., None]], axis=-1)
    sol = lax.linalg.triangular_solve(m, rhs, left_side=True, lower=True, unit_diagonal=True)
    u_c, w_c = sol[..., :dv], sol[..., dv:]
    a_in = jnp.einsum('bnhid,bnhjd->bnhij', q, k) * gamma
    q_dec = q * jnp.exp(gc)[..., None]
    k_dec = k * jnp.exp(gc[..., -1:] - gc)[..., None]
    chunk_dec = jnp.exp(gc[..., -1])

    def step(state, xs):
        u_i, w_i, a_i, qd_i, kd_i, d_i = xs
        v_new = u_i - jnp.einsum('bhck,bhkv->bhcv', w_i, state)
        o_i = jnp.einsum('bhck,bhkv->bhcv', qd_i, state) + jnp.einsum('bhcj,bhjv->bhcv', a_i, v_new)
        state = state * d_i[..., None, None] + jnp.einsum('bhck,bhcv->bhkv', kd_i, v_new)
        return state, o_i

    xs = tuple(jnp.moveaxis(t, 1, 0) for t in (u_c, w_c, a_in, q_dec, k_dec, chunk_dec))
    _, o = lax.scan(step, jnp.zeros((b, h, dk, dv), jnp.float32), xs)
    return jnp.moveaxis(o, 0, 1).swapaxes(2, 3).reshape(b, s, h, dv)

def gdn_branch(z, conv_w, a_log, dt_bias, norm_g):
    b, s, _ = z.shape
    qkv, b_logit, a_logit, gate = split_cols_2(z, GDN_IN_SIZES)
    qkv = jax.nn.silu(causal_depthwise_conv(qkv, conv_w))
    q, k, v = split_cols_2(qkv, (GDN_HEADS * GDN_K_DIM, GDN_HEADS * GDN_K_DIM, GDN_HEADS * GDN_V_DIM))
    q = l2_normalize(heads(q, GDN_HEADS)) * (GDN_K_DIM ** -0.5)
    k = l2_normalize(heads(k, GDN_HEADS))
    v = heads(v, GDN_HEADS).astype(jnp.float32)
    beta = jax.nn.sigmoid(b_logit.astype(jnp.float32))
    g = -jnp.exp(a_log.astype(jnp.float32)) * jax.nn.softplus(a_logit.astype(jnp.float32) + dt_bias)
    o = chunk_gated_delta_rule(q, k, v, g, beta)
    o = rms_norm(o, norm_g) * jax.nn.silu(heads(gate, GDN_HEADS).astype(jnp.float32))
    return o.reshape(b, s, GDN_WIDTH).astype(z.dtype)

def swiglu(x, w_gate, w_up, w_down):
    return (jax.nn.silu(x @ w_gate) * (x @ w_up)) @ w_down

def moe_swiglu(x2d, w_router, w_gate, w_up, w_down):
    n_tok, d = x2d.shape
    n_assign = n_tok * TOP_K
    n_blocks = -(-(n_assign + N_EXPERTS * (MOE_BLOCK - 1)) // MOE_BLOCK)
    logits = jnp.dot(x2d, w_router).astype(jnp.float32)
    top_logits, top_e = lax.top_k(logits, TOP_K)
    top_w = jax.nn.softmax(top_logits, axis=-1).reshape(-1)
    flat_e = top_e.reshape(-1)
    order = jnp.argsort(flat_e)
    e_sorted = flat_e[order]
    tok_sorted = order // TOP_K
    w_sorted = top_w[order]
    counts = jnp.bincount(flat_e, length=N_EXPERTS)
    padded = (counts + MOE_BLOCK - 1) // MOE_BLOCK * MOE_BLOCK
    pad_end = jnp.cumsum(padded)
    rank = jnp.arange(n_assign) - (jnp.cumsum(counts) - counts)[e_sorted]
    dest = (pad_end - padded)[e_sorted] + rank
    rows = jnp.zeros((n_blocks * MOE_BLOCK, d), x2d.dtype).at[dest].set(x2d[tok_sorted])
    block_e = jnp.minimum(jnp.searchsorted(pad_end, jnp.arange(n_blocks) * MOE_BLOCK, side='right'), N_EXPERTS - 1)

    def expert_block(args):
        xb, e = args
        return (jax.nn.silu(xb @ w_gate[e]) * (xb @ w_up[e])) @ w_down[e]

    y_rows = lax.map(expert_block, (rows.reshape(n_blocks, MOE_BLOCK, d), block_e)).reshape(n_blocks * MOE_BLOCK, d)
    y = jax.ops.segment_sum(y_rows[dest] * w_sorted[:, None], tok_sorted, num_segments=n_tok)
    return y.astype(x2d.dtype)

def second_inputs(seed: int = 0) -> dict:
    key = jax.random.key(seed)
    ks = iter(jax.random.split(key, 64))
    f32 = jnp.float32
    L = DEPTH
    LD = (DEPTH + 1) // 2
    LM = DEPTH // 2
    LV = DEPTH - 1

    def nrm(shape, scale):
        return jax.random.normal(next(ks), shape, f32) * scale

    def unif(shape, lo, hi):
        return jax.random.uniform(next(ks), shape, f32, lo, hi)

    def gain(shape):
        return 1.0 + nrm(shape, 0.02)

    x = nrm((BATCH, SEQ, D_MODEL), 1.0)
    p = nrm((DEPTH, BATCH, SEQ, PLE_DIM), 1.0)
    positions = (jnp.arange(SEQ, dtype=jnp.int32)[None, :]
                 + jax.random.randint(next(ks), (BATCH, 1), 0, 1024, dtype=jnp.int32))
    dt = jnp.exp(unif((L, GDN_HEADS), math.log(1e-3), math.log(1e-1)))
    gdn_dt_bias = dt + jnp.log(-jnp.expm1(-dt))
    return {
        'x': x,
        'p': p,
        'positions': positions,
        'norm_mix_g': gain((L, D_MODEL)),
        'w_in': nrm((L, D_MODEL, N_IN), D_MODEL ** -0.5),
        'rwkv_mu': unif((L, RWKV_IN), 0.0, 1.0),
        'rwkv_w0': unif((L, RWKV_WIDTH), -6.0, 1.0),
        'rwkv_w_up': nrm((L, DECAY_LORA, RWKV_WIDTH), DECAY_LORA ** -0.5),
        'rwkv_a0': unif((L, RWKV_WIDTH), -1.0, 1.0),
        'rwkv_a_up': nrm((L, ICLR_LORA, RWKV_WIDTH), ICLR_LORA ** -0.5),
        'rwkv_g_up': nrm((L, GATE_LORA, RWKV_WIDTH), GATE_LORA ** -0.5),
        'rwkv_k_k': 0.85 + nrm((L, RWKV_WIDTH), 0.05),
        'rwkv_k_a': 1.0 + nrm((L, RWKV_WIDTH), 0.05),
        'rwkv_r_k': nrm((L, RWKV_HEADS, RWKV_HEAD_DIM), 0.1),
        'rwkv_ln_g': gain((L, RWKV_WIDTH)),
        'rwkv_ln_b': nrm((L, RWKV_WIDTH), 0.02),
        'vres_mu': unif((LV, D_MODEL), 0.0, 1.0),
        'vres_down': nrm((LV, D_MODEL, VRES_LORA), D_MODEL ** -0.5),
        'vres_up': nrm((LV, VRES_LORA, RWKV_WIDTH), VRES_LORA ** -0.5),
        'vres_b': 1.0 + nrm((LV, RWKV_WIDTH), 0.1),
        'mla_q_norm_g': gain((L, Q_LORA_RANK)),
        'mla_kv_norm_g': gain((L, KV_LORA_RANK)),
        'mla_w_uq': nrm((L, Q_LORA_RANK, MLA_HEADS * MLA_QK_DIM), Q_LORA_RANK ** -0.5),
        'mla_w_ukv': nrm((L, KV_LORA_RANK, MLA_HEADS * (QK_NOPE_DIM + MLA_V_DIM)), KV_LORA_RANK ** -0.5),
        'mla_qk_norm_q': gain((L, MLA_QK_DIM)),
        'mla_qk_norm_k': gain((L, MLA_QK_DIM)),
        'gdn_conv_w': nrm((L, GDN_CONV, GDN_QKV), GDN_CONV ** -0.5),
        'gdn_a_log': jnp.log(unif((L, GDN_HEADS), 1.0, 16.0)),
        'gdn_dt_bias': gdn_dt_bias,
        'gdn_norm_g': gain((L, GDN_V_DIM)),
        'w_br_rwkv': nrm((L, RWKV_WIDTH, D_MODEL), RWKV_WIDTH ** -0.5),
        'w_br_mla': nrm((L, MLA_WIDTH, D_MODEL), MLA_WIDTH ** -0.5),
        'w_br_gdn': nrm((L, GDN_WIDTH, D_MODEL), GDN_WIDTH ** -0.5),
        'w_out': nrm((L, D_MODEL, D_MODEL), D_MODEL ** -0.5),
        'norm_ffn_g': gain((L, D_MODEL)),
        'ffn_wg': nrm((LD, D_MODEL, FF_DENSE), D_MODEL ** -0.5),
        'ffn_wu': nrm((LD, D_MODEL, FF_DENSE), D_MODEL ** -0.5),
        'ffn_wd': nrm((LD, FF_DENSE, D_MODEL), FF_DENSE ** -0.5),
        'moe_router': nrm((LM, D_MODEL, N_EXPERTS), D_MODEL ** -0.5),
        'moe_wg': nrm((LM, N_EXPERTS, D_MODEL, FF_EXPERT), D_MODEL ** -0.5),
        'moe_wu': nrm((LM, N_EXPERTS, D_MODEL, FF_EXPERT), D_MODEL ** -0.5),
        'moe_wd': nrm((LM, N_EXPERTS, FF_EXPERT, D_MODEL), FF_EXPERT ** -0.5),
        'ple_proj': nrm((L, PLE_DIM, D_MODEL), PLE_DIM ** -0.5),
        'ple_gate': nrm((L, D_MODEL, D_MODEL), D_MODEL ** -0.5),
        'ple_norm_g': gain((L, D_MODEL)),
    }

def second_block(x, p, positions, norm_mix_g, w_in, rwkv_mu, rwkv_w0, rwkv_w_up, rwkv_a0, rwkv_a_up,
              rwkv_g_up, rwkv_k_k, rwkv_k_a, rwkv_r_k, rwkv_ln_g, rwkv_ln_b, vres_mu, vres_down,
              vres_up, vres_b, mla_q_norm_g, mla_kv_norm_g, mla_w_uq, mla_w_ukv, mla_qk_norm_q,
              mla_qk_norm_k, gdn_conv_w, gdn_a_log, gdn_dt_bias, gdn_norm_g, w_br_rwkv, w_br_mla,
              w_br_gdn, w_out, norm_ffn_g, ffn_wg, ffn_wu, ffn_wd, moe_router, moe_wg, moe_wu, moe_wd,
              ple_proj, ple_gate, ple_norm_g):
    b, s, d = x.shape
    cos, sin = rope_tables_2(positions)
    h = x
    v_first = None
    for i in range(DEPTH):
        u = rms_norm(h, norm_mix_g[i])
        z = u @ w_in[i]
        z_rwkv, z_mla, z_gdn, z_gate = split_cols_2(z, (RWKV_IN, MLA_IN, GDN_IN, GATE_IN))
        vres = None if i == 0 else (vres_mu[i - 1], vres_down[i - 1], vres_up[i - 1], vres_b[i - 1])
        o_a, v_first = rwkv7_branch(z_rwkv, u, v_first, vres, rwkv_mu[i], rwkv_w0[i], rwkv_w_up[i],
                                    rwkv_a0[i], rwkv_a_up[i], rwkv_g_up[i], rwkv_k_k[i], rwkv_k_a[i],
                                    rwkv_r_k[i], rwkv_ln_g[i], rwkv_ln_b[i])
        o_b = mla_branch(z_mla, cos, sin, mla_q_norm_g[i], mla_kv_norm_g[i], mla_w_uq[i], mla_w_ukv[i],
                         mla_qk_norm_q[i], mla_qk_norm_k[i])
        o_c = gdn_branch(z_gdn, gdn_conv_w[i], gdn_a_log[i], gdn_dt_bias[i], gdn_norm_g[i])
        g_a, g_b, g_c = jnp.split(jax.nn.sigmoid(z_gate), N_BRANCH, axis=-1)
        merged = (g_a * (o_a @ w_br_rwkv[i]) + g_b * (o_b @ w_br_mla[i])
                  + g_c * (o_c @ w_br_gdn[i]))
        h = h + merged @ w_out[i]
        u2 = rms_norm(h, norm_ffn_g[i])
        if i % 2 == 0:
            f = swiglu(u2, ffn_wg[i // 2], ffn_wu[i // 2], ffn_wd[i // 2])
        else:
            f = moe_swiglu(u2.reshape(b * s, d), moe_router[i // 2], moe_wg[i // 2],
                           moe_wu[i // 2], moe_wd[i // 2]).reshape(b, s, d)
        h = h + f
        e = rms_norm(p[i] @ ple_proj[i], ple_norm_g[i])
        h = h + jax.nn.sigmoid(h @ ple_gate[i]) * e
    return h


def setup_inputs(seed=0):
    out = dict(first_inputs(seed))
    for name, value in second_inputs(seed + 1).items():
        if name != "x":
            out[name + "_2"] = value
    return out


def reference(
    x, positions, ffn1_norm, ffn1_w_gate, ffn1_w_up, ffn1_w_down, mix_norm, ffn2_norm,
    ffn2_w_gate, ffn2_w_up, ffn2_w_down, ev_w_in, ev_sgu_norm, ev_sgu_w, ev_sgu_b, ev_cmp_pos_k,
    ev_cmp_w1_k, ev_cmp_w2_k, ev_cmp_pos_v, ev_cmp_w1_v, ev_cmp_w2_v, ev_w_out, od_w_in,
    od_w_out, final_norm, p_2, positions_2, norm_mix_g_2, w_in_2, rwkv_mu_2, rwkv_w0_2,
    rwkv_w_up_2, rwkv_a0_2, rwkv_a_up_2, rwkv_g_up_2, rwkv_k_k_2, rwkv_k_a_2, rwkv_r_k_2,
    rwkv_ln_g_2, rwkv_ln_b_2, vres_mu_2, vres_down_2, vres_up_2, vres_b_2, mla_q_norm_g_2,
    mla_kv_norm_g_2, mla_w_uq_2, mla_w_ukv_2, mla_qk_norm_q_2, mla_qk_norm_k_2, gdn_conv_w_2,
    gdn_a_log_2, gdn_dt_bias_2, gdn_norm_g_2, w_br_rwkv_2, w_br_mla_2, w_br_gdn_2, w_out_2,
    norm_ffn_g_2, ffn_wg_2, ffn_wu_2, ffn_wd_2, moe_router_2, moe_wg_2, moe_wu_2, moe_wd_2,
    ple_proj_2, ple_gate_2, ple_norm_g_2,
):
    x = first_block(
        x, positions, ffn1_norm, ffn1_w_gate, ffn1_w_up, ffn1_w_down, mix_norm, ffn2_norm,
        ffn2_w_gate, ffn2_w_up, ffn2_w_down, ev_w_in, ev_sgu_norm, ev_sgu_w, ev_sgu_b,
        ev_cmp_pos_k, ev_cmp_w1_k, ev_cmp_w2_k, ev_cmp_pos_v, ev_cmp_w1_v, ev_cmp_w2_v,
        ev_w_out, od_w_in, od_w_out, final_norm,
    )
    return second_block(
        x, p_2, positions_2, norm_mix_g_2, w_in_2, rwkv_mu_2, rwkv_w0_2, rwkv_w_up_2, rwkv_a0_2,
        rwkv_a_up_2, rwkv_g_up_2, rwkv_k_k_2, rwkv_k_a_2, rwkv_r_k_2, rwkv_ln_g_2, rwkv_ln_b_2,
        vres_mu_2, vres_down_2, vres_up_2, vres_b_2, mla_q_norm_g_2, mla_kv_norm_g_2,
        mla_w_uq_2, mla_w_ukv_2, mla_qk_norm_q_2, mla_qk_norm_k_2, gdn_conv_w_2, gdn_a_log_2,
        gdn_dt_bias_2, gdn_norm_g_2, w_br_rwkv_2, w_br_mla_2, w_br_gdn_2, w_out_2, norm_ffn_g_2,
        ffn_wg_2, ffn_wu_2, ffn_wd_2, moe_router_2, moe_wg_2, moe_wu_2, moe_wd_2, ple_proj_2,
        ple_gate_2, ple_norm_g_2,
    )


_drawn_inputs = setup_inputs


def setup_inputs(seed=0):
    import zlib

    import numpy as np

    out = dict(_drawn_inputs(seed))
    spreads = {}
    factors = {'rwkv_ln_g_2': 4.416,
     'rwkv_ln_b_2': 2.934,
     'vres_b_2': 81.53,
     'mla_q_norm_g_2': 8.0,
     'mla_kv_norm_g_2': 5.687,
     'mla_qk_norm_q_2': 8.0,
     'mla_qk_norm_k_2': 8.0,
     'gdn_norm_g_2': 3.225,
     'vres_mu_2': 8.0,
     'vres_down_2': 4.417,
     'vres_up_2': 4.374,
     'ple_norm_g_2': 2.668}
    for name, (base, spread) in spreads.items():
        noise = np.random.default_rng([zlib.crc32(name.encode()), seed]).standard_normal(out[name].shape)
        drawn = base * np.exp(spread * noise) if base else spread * noise
        out[name] = jnp.asarray(drawn.astype(out[name].dtype))
    for name, factor in factors.items():
        out[name] = (out[name] * factor).astype(out[name].dtype)
    return out
```

```python
from contextlib import ExitStack

import numpy as np

import concourse.bass as bass
from concourse import mybir

F32 = mybir.dt.float32
BF16 = mybir.dt.bfloat16
I32 = mybir.dt.int32
U32 = mybir.dt.uint32
ALU = mybir.AluOpType
ACT = mybir.ActivationFunctionType
AX = mybir.AxisListType.X

P = 128
S = 256
TB = S // P
D = 1024
KT = D // P
HD = 64
BANK = 512
GROUP = 256
UNIT = KT * GROUP
RING = 9 * UNIT
BIG = 1e30
EPS = 1e-6


def constant_table():
    r = np.arange(P)
    row, col = r[:, None], r[None, :]
    parts = {}
    parts["ident"] = (row == col)
    parts["zero"] = np.zeros((P, P))
    parts["hide"] = np.where(col > row, BIG, 0.0)
    parts["incl"] = (row <= col)
    parts["strict"] = (row < col)
    parts["after"] = (row > col)
    for level in range(7):
        b = 1 << level
        parts[f"level{level}"] = ((row // (2 * b) == col // (2 * b)) & (row // b % 2 == 0) & (col // b % 2 == 1))
    parts["head_ones"] = (row // HD == col // HD)
    parts["head_pick"] = (row // HD == r[None, :2])
    n_cmp = 15
    t = (np.arange(TB)[:, None, None] * P + r[None, :, None]).transpose(1, 0, 2)
    end = np.arange(n_cmp)[None, None, :] * 16 + 31
    parts["cmp_hide"] = np.where(end <= t, 0.0, BIG).reshape(P, -1)
    parts["cmp_any"] = (t >= 31).reshape(P, -1)
    rope = lambda theta, n: np.float32(theta) ** (-np.arange(0, n, 2, dtype=np.float32) / np.float32(n))
    parts["freq"] = np.broadcast_to(np.concatenate([rope(500000.0, 16), rope(500000.0, 8)]), (P, 12))
    parts["freq2"] = np.broadcast_to(np.float32(1) / (np.float32(10000.0) ** (np.arange(0, 32, 2, dtype=np.float32) / np.float32(32))), (P, 16))
    parts["iota"] = np.broadcast_to(np.arange(P), (P, P))
    parts["ones"] = np.ones((P, P))
    where, at = {}, 0
    for name, a in parts.items():
        parts[name] = np.asarray(a, np.float32).reshape(P, -1)
        where[name] = (at, parts[name].shape[1])
        at += parts[name].shape[1]
    return np.ascontiguousarray(np.concatenate(list(parts.values()), axis=1)), where


def columns(v):
    return np.asarray(v).reshape(-1, P).T


def column_table(inp):
    parts = {}
    for name in ("ffn1_norm", "mix_norm", "ffn2_norm", "norm_mix_g_2", "norm_ffn_g_2"):
        for i in range(2):
            parts[f"{name}{i}"] = columns(inp[name][i])
    for i in range(2):
        for name in ("rwkv_mu_2", "rwkv_w0_2", "rwkv_a0_2", "rwkv_k_k_2", "rwkv_k_a_2", "rwkv_r_k_2",
                     "mla_q_norm_g_2", "mla_kv_norm_g_2", "gdn_conv_w_2"):
            parts[f"{name}{i}"] = columns(inp[name][i])
    parts["vres_mu_2"] = columns(inp["vres_mu_2"][0])
    parts["vres_b_2"] = columns(inp["vres_b_2"][0])
    pos = np.asarray(inp["ev_cmp_pos_k"][0]), np.asarray(inp["ev_cmp_pos_v"][0])
    for name, a in zip(("cmp_pos_k", "cmp_pos_v"), pos):
        parts[name] = a.reshape(16, 2 * HD).T
    parts["sgu_b"] = np.asarray(inp["ev_sgu_b"][0]).T
    where, at = {}, 0
    for name, a in parts.items():
        where[name] = (at, a.shape[1])
        at += a.shape[1]
    return np.ascontiguousarray(np.concatenate([np.asarray(a) for a in parts.values()], axis=1)), where


def row_table(inp):
    parts = {"sgu_norm": inp["ev_sgu_norm"][0], "final_norm": inp["final_norm"]}
    for i in range(2):
        for name in ("rwkv_ln_g_2", "rwkv_ln_b_2", "mla_qk_norm_q_2", "mla_qk_norm_k_2", "gdn_norm_g_2",
                     "gdn_a_log_2", "gdn_dt_bias_2", "ple_norm_g_2"):
            parts[f"{name}{i}"] = inp[name][i]
    where, at = {}, 0
    for name, a in parts.items():
        where[name] = (at, np.asarray(a).size)
        at += np.asarray(a).size
    return np.ascontiguousarray(np.concatenate([np.asarray(a).ravel() for a in parts.values()])[None]), where


def pack(w):
    w = np.asarray(w)
    return w.reshape(-1, P, w.shape[1]).transpose(1, 0, 2)


def pack_chunks(w, widths):
    out, at = [], 0
    for n in widths:
        out.append(np.ascontiguousarray(pack(np.asarray(w)[:, at:at + n])).ravel())
        at += n
    assert at == w.shape[1]
    return np.concatenate(out)


def pack_ffn(gate, up, down, size=GROUP):
    n, unit = gate.shape[1] // size, KT * size
    out = np.empty((n, P, 3, unit), np.float32)
    out[:, :, 0] = np.asarray(gate).reshape(KT, P, n, size).transpose(2, 1, 0, 3).reshape(n, P, unit)
    out[:, :, 1] = np.asarray(up).reshape(KT, P, n, size).transpose(2, 1, 0, 3).reshape(n, P, unit)
    out[:, :, 2] = np.asarray(down).reshape(n, size // P, P, D).transpose(0, 2, 1, 3).reshape(n, P, unit)
    return out.reshape(n, P, 3 * unit)


EVEN_CHUNKS = [512] * 4 + [420]
ODD_CHUNKS = [512] * 4 + [292]
OUT_CHUNKS = [512] * 2
FEAT_CHUNKS = [512] * 6 + [256]
TOK_CHUNKS = [432, 512]
RWKV_IN, MLA_IN, GDN_QKV = 1792, 416, 1536


def gate_branch_chunks(w_gate, branches):
    out = []
    for j in range(2):
        for x in range(3):
            out.append(pack_chunks(w_gate[:, x * D + j * 512:x * D + j * 512 + 512], [512]))
            out.append(pack_chunks(branches[x][:, j * 512:j * 512 + 512], [512]))
    return np.concatenate(out)


def lay_out(inp):
    g = {k: np.asarray(v) for k, v in inp.items()}
    a = {}
    a["x"] = g["x"].reshape(TB, P, D).transpose(1, 0, 2).reshape(P, TB * D)
    a["positions"] = np.concatenate([g["positions"].reshape(TB, P).T, g["positions_2"].reshape(TB, P).T], axis=1)
    a["consts"] = constant_table()[0]
    a["cols"] = column_table(g)[0]
    a["rows"] = row_table(g)[0]
    ffn = []
    for i in range(2):
        ffn.append(pack_ffn(g["ffn1_w_gate"][i], g["ffn1_w_up"][i], g["ffn1_w_down"][i]))
        ffn.append(pack_ffn(g["ffn2_w_gate"][i], g["ffn2_w_up"][i], g["ffn2_w_down"][i]))
    ffn.append(pack_ffn(g["ffn_wg_2"][0], g["ffn_wu_2"][0], g["ffn_wd_2"][0]))
    a["ffn_w"] = np.concatenate(ffn)
    a["moe_w"] = np.concatenate([pack_ffn(g["moe_wg_2"][0, e], g["moe_wu_2"][0, e], g["moe_wd_2"][0, e], P) for e in range(8)])
    a["ev_in_w"] = pack_chunks(g["ev_w_in"][0], EVEN_CHUNKS)
    a["ev_out_w"] = pack_chunks(g["ev_w_out"][0], OUT_CHUNKS)
    a["od_in_w"] = pack_chunks(g["od_w_in"][0], ODD_CHUNKS)
    a["od_out_w"] = pack_chunks(g["od_w_out"][0], OUT_CHUNKS)
    a["sgu_wT"] = g["ev_sgu_w"][0].transpose(2, 0, 1).reshape(P, -1)
    a["cmp_w1"] = np.concatenate([pack(g[f"ev_cmp_w1_{x}"][0]).reshape(P, -1) for x in "kv"], axis=1)
    w2k, w2v = (pack(g[f"ev_cmp_w2_{x}"][0]) for x in "kv")
    a["cmp_w2"] = np.concatenate([np.concatenate([w2k, w2k], axis=2).reshape(P, -1), w2v.reshape(P, -1)], axis=1)
    for i in range(2):
        w = g["w_in_2"][i]
        c = np.cumsum([0, RWKV_IN, MLA_IN, GDN_QKV, 16, 512, 3 * D])
        a[f"feat_w{i}"] = pack_chunks(np.concatenate([w[:, c[0]:c[1]], w[:, c[2]:c[3]]], axis=1), FEAT_CHUNKS)
        a[f"tok_w{i}"] = pack_chunks(np.concatenate([w[:, c[1]:c[2]], w[:, c[3]:c[4]], w[:, c[4]:c[5]]], axis=1), TOK_CHUNKS)
        a[f"merge_w{i}"] = gate_branch_chunks(w[:, c[5]:c[6]], [g[f"w_br_{b}_2"][i] for b in ("rwkv", "mla", "gdn")])
        a[f"out_w{i}"] = pack_chunks(g["w_out_2"][i], OUT_CHUNKS)
        a[f"lora_up{i}"] = np.concatenate([np.concatenate([g["rwkv_w_up_2"][i], g["rwkv_a_up_2"][i]], axis=0), g["rwkv_g_up_2"][i]], axis=1)
        a[f"mla_up{i}"] = np.concatenate([pack(g["mla_w_uq_2"][i]).reshape(P, -1), g["mla_w_ukv_2"][i]], axis=1)
        a[f"ple_proj{i}"] = pack(g["ple_proj_2"][i]).reshape(P, -1)
        a[f"ple_gate{i}"] = pack_chunks(g["ple_gate_2"][i], OUT_CHUNKS)
        a[f"pT{i}"] = g["p_2"][i, 0].T.reshape(2, P, S).transpose(1, 0, 2).reshape(P, -1)
    a["vres_down"] = pack(g["vres_down_2"][0]).reshape(P, -1)
    a["vres_up"] = g["vres_up_2"][0]
    a["router"] = pack(g["moe_router_2"][0]).reshape(P, -1)
    return {k: np.ascontiguousarray(v) for k, v in a.items()}


class Program:

    def __init__(self, nc, inp, tables):
        self.nc, self.inp = nc, inp
        self.const_at, self.col_at, self.row_at = tables
        self.ctx = ExitStack()
        self.n_phases = 0
        self.before = None
        sb = lambda name, n: self.ctx.enter_context(nc.sbuf_tensor(name, [P, n], F32))
        self.ring = sb("ring", RING)
        self.x_sb = sb("x_resid", TB * D)
        self.xT_sb = sb("xT_norm", KT * S)
        self.consts = sb("constants", inp["consts"].shape[1])
        self.cols = sb("columns", inp["cols"].shape[1])
        self.rope = sb("rope_tables", 2 * TB * (8 + 4 + 16))
        free = (nc.sbuf_bytes_remaining if not callable(nc.sbuf_bytes_remaining) else nc.sbuf_bytes_remaining())
        self.arena_size = free // 4 - 64
        self.arena = sb("arena", self.arena_size)
        self.psum = self.ctx.enter_context(nc.psum_tensor("psum", [P, 8, BANK], F32))
        self.x = self.x_sb[:].rearrange("p (b d) -> p b d", b=TB)
        self.xT = self.xT_sb[:].rearrange("p (k t) -> p k t", k=KT)
        self.small_loaded = self.ctx.enter_context(nc.semaphore("small_loaded"))
        self.n_small = 0
        self.slot_loaded = [self.ctx.enter_context(nc.semaphore(f"slot_loaded_{i}")) for i in range(4)]
        self.n_slot = [0] * 4
        self.ident = self.const("ident")

    def const(self, name):
        at, n = self.const_at[name]
        return self.consts[:, at:at + n]

    def col(self, name):
        at, n = self.col_at[name]
        return self.cols[:, at:at + n]

    def load(self, dst, src):
        self.nc.sync.dma_start(dst, src).then_inc(self.small_loaded, 16)
        self.n_small += 1

    def load_row(self, dst, name):
        at, n = self.row_at[name]
        self.load(dst, self.inp["rows"][0:1, at:at + n].to_broadcast([P, n]))

    def wait_small(self, eng):
        eng.wait_ge(self.small_loaded, 16 * self.n_small)

    def phase(self):
        return Phase(self)

    def solo(self, engine, steps):
        with self.phase() as ph:
            step_done = ph.semaphore("step_done")

            def program(eng):
                self.wait_small(eng)
                steps(Steps(eng, step_done))
            {"vector": ph.block.vector, "scalar": ph.block.scalar, "gpsimd": ph.block.gpsimd}[engine](program)


class Phase:

    def __init__(self, prog):
        self.prog = prog

    def __enter__(self):
        if self.prog.before is not None:
            for s in self.prog.before.sems:
                self.prog.nc.gpsimd.sem_clear(s)
        self.ctx = ExitStack()
        self.prog.n_phases += 1
        self.number = self.prog.n_phases
        self.sems = []
        self.block_ctx = self.prog.nc.Block(no_gpsimd_drain=True)
        self.block = self.block_ctx.__enter__()
        return self

    def semaphore(self, name):
        s = self.ctx.enter_context(self.prog.nc.semaphore(f"{name}_{self.number}"))
        self.sems.append(s)
        return s

    def __exit__(self, *e):
        self.block_ctx.__exit__(*e)
        if self.prog.before is not None:
            self.prog.before.ctx.close()
        self.prog.before = self


class Steps:

    def __init__(self, eng, sem):
        self.eng, self.sem, self.n = eng, sem, 0

    def __call__(self, *instructions):
        for ins in instructions:
            ins.then_inc(self.sem, 1)
        self.n += len(instructions)
        self.eng.wait_ge(self.sem, self.n)


class Arena:

    def __init__(self, prog, at=0):
        self.prog, self.at = prog, at

    def take(self, *shape, align=1):
        n = int(np.prod(shape))
        assert self.at + n <= self.prog.arena_size, ("arena", self.at, n, self.prog.arena_size)
        v = self.prog.arena[:, self.at:self.at + n]
        self.at += n
        if len(shape) == 1:
            return v
        names = "abcd"[:len(shape)]
        kw = {names[i]: shape[i] for i in range(len(shape) - 1)}
        return v.rearrange(f"p ({' '.join(names)}) -> p {' '.join(names)}", **kw)


def spread(ap, *shape):
    return ap.to_broadcast([ap.shape[0], *shape])


class Weights:

    def __init__(self, prog, pieces, slots, slot_floats):
        self.prog, self.pieces, self.slots, self.size = prog, pieces, slots, slot_floats
        self.ahead = 0

    def buffer(self, i):
        n = self.pieces[i].shape[1]
        at = i % self.slots * self.size
        return self.prog.ring[:, at:at + n]

    def start(self, eng, i):
        s = i % self.slots
        eng.dma_start(self.buffer(i), self.pieces[i]).then_inc(self.prog.slot_loaded[s], 16)
        self.prog.n_slot[s] += 1

    def prefetch(self):
        self.base = list(self.prog.n_slot)
        self.ahead = min(self.slots, len(self.pieces))
        for i in range(self.ahead):
            self.start(self.prog.nc.sync, i)

    def wait(self, eng, i):
        s = i % self.slots
        eng.wait_ge(self.prog.slot_loaded[s], 16 * (self.base[s] + i // self.slots + 1))

    def rest(self, eng, used, per_piece):
        for i in range(self.ahead, len(self.pieces)):
            eng.wait_ge(used, per_piece * (i - self.slots + 1))
            self.start(eng, i)


def chunk_weights(prog, flat, widths, kt=KT):
    pieces, at = [], 0
    for n in widths:
        pieces.append(flat[at:at + P * kt * n].rearrange("(p c) -> p c", p=P))
        at += P * kt * n
    return Weights(prog, pieces, 4, KT * 512)


def transposes(prog, sources, dst, width=P, gains=None):
    n = len(sources)
    banks = [(b, min(4, n - 4 * b)) for b in range(-(-n // 4))]
    with prog.phase() as ph:
        bank_full, emptied = ph.semaphore("bank_full"), [ph.semaphore("emptied_by_scalar"), ph.semaphore("emptied_by_vector")]

        @ph.block.tensor
        def _(pe):
            prog.wait_small(pe)
            for b, m in banks:
                if b >= 8:
                    pe.wait_ge(emptied[b % 2], (b - 8) // 2 + 1)
                for j in range(m):
                    last = pe.transpose(prog.psum[0:width, b % 8, j * P:(j + 1) * P], sources[4 * b + j],
                                        prog.ident)
                last.then_inc(bank_full, 1)

        def empty(eng, which, scale):
            prog.wait_small(eng)
            for b, m in banks:
                if b % 2 != which:
                    continue
                eng.wait_ge(bank_full, b + 1)
                if gains is None:
                    last = scale(dst[0:width, 4 * b * P:(4 * b + m) * P], prog.psum[0:width, b % 8, 0:m * P], 1.0)
                else:
                    for j in range(0, m, 2):
                        i = 4 * b + j
                        last = scale(dst[:, i * P:(i + 2) * P], prog.psum[:, b % 8, j * P:(j + 2) * P],
                                     gains[:, i // 2:i // 2 + 1])
                last.then_inc(emptied[which], 1)

        @ph.block.scalar
        def _(act):
            empty(act, 0, lambda o, i, s: act.activation(o, i, ACT.Copy, scale=s))

        @ph.block.vector
        def _(dve):
            empty(dve, 1, lambda o, i, s: dve.tensor_scalar(o, i, s, None, ALU.mult))


def row_scales(prog, x, width, scale_out, work, eps=EPS):
    with prog.phase() as ph:
        squared, rooted, ready = ph.semaphore("squared"), ph.semaphore("rooted"), ph.semaphore("ready")

        @ph.block.scalar
        def _(act):
            prog.wait_small(act)
            for b in range(TB):
                act.activation(work[:, b, :], x[:, b, :], ACT.Square, accum_out=scale_out[:, b:b + 1]).then_inc(squared, 1)
            act.wait_ge(ready, 1)
            act.activation(scale_out, scale_out, ACT.Sqrt).then_inc(rooted, 1)

        @ph.block.vector
        def _(dve):
            dve.wait_ge(squared, TB)
            dve.tensor_scalar(scale_out, scale_out, 1.0 / width, eps, ALU.mult, ALU.add).then_inc(ready, 1)
            dve.wait_ge(rooted, 1)
            dve.reciprocal(scale_out, scale_out).then_inc(ready, 1)


def norm_transposed(prog, gain, at=0):
    mem = Arena(prog, at)
    xn, scale = mem.take(TB, D), mem.take(TB)
    row_scales(prog, prog.x, D, scale, xn)
    with prog.phase() as ph:
        scaled = ph.semaphore("scaled")

        @ph.block.vector
        def _(dve):
            dve.tensor_scalar(xn[:, 0, :], prog.x[:, 0, :], scale[:, 0:1], None, ALU.mult).then_inc(scaled, 1)

        @ph.block.scalar
        def _(act):
            act.activation(xn[:, 1, :], prog.x[:, 1, :], ACT.Copy, scale=scale[:, 1:2]).then_inc(scaled, 1)
    transposes(prog, [xn[:, b, k * P:(k + 1) * P] for k in range(KT) for b in range(TB)], prog.xT_sb[:], gains=gain)


def feed_forward(prog, weights, total, factor=1.0):
    mem = Arena(prog)
    hidden, silu = mem.take(2, S), mem.take(2, S)
    zeros = prog.const("zero")
    slots = weights.slots
    acc = lambda tb, half: prog.psum[:, 4 + 2 * tb + half, :]
    loops = total // slots
    with prog.phase() as ph:
        tile_ready, silu_ready, hidden_ready = ph.semaphore("tile_ready"), ph.semaphore("silu_ready"), ph.semaphore("hidden_ready")
        group_used = ph.semaphore("group_used")

        @ph.block.sync
        def _(sp):
            def load(g, slot, wait_for):
                sp.wait_ge(group_used, wait_for)
                sp.dma_start(weights.buffer(slot), weights.stream[bass.ds(g, 1), :, :].rearrange("g p c -> p (g c)")
                             if not isinstance(g, int) else weights.stream[g]).then_inc(prog.slot_loaded[slot], 16)

            with sp.Fori(0, (total - slots) // slots) as it:
                for s in range(slots):
                    load(weights.first + slots + it * slots + s, s, it * slots + s + 1)
            for g in range((total - slots) // slots * slots + slots, total):
                load(weights.first + g, g % slots, g - slots + 1)

            for g in range(slots, total):
                prog.n_slot[g % slots] += 1

        @ph.block.tensor
        def _(pe):
            for b in range(4):
                pe.matmul(prog.psum[:, 4 + b, :], zeros[:, 0:64].bitcast(BF16), zeros_wide(prog), start=True,
                          stop=False, skip_group_check=True)

            def group(slot, loaded, tile0):
                pe.wait_ge(prog.slot_loaded[slot], loaded)
                w = prog.ring[:, slot * 3 * UNIT:(slot + 1) * 3 * UNIT].rearrange("p (m u) -> p m u", m=3)
                gate, up = (w[:, m, :].rearrange("p (k f) -> p k f", k=KT) for m in (0, 1))
                down = w[:, 2, :].rearrange("p (t n) -> p t n", t=2)
                for t in range(2):
                    for m, wm in enumerate((gate, up)):
                        for k in range(KT):
                            last = pe.matmul(prog.psum[:, t, m * S:(m + 1) * S], wm[:, k, t * P:(t + 1) * P],
                                             prog.xT[:, k, :], start=(k == 0), stop=(k == KT - 1))
                    last.then_inc(tile_ready, 1)
                for t in range(2):
                    pe.wait_ge(hidden_ready, tile0 + t + 1)
                    for tb in range(TB):
                        for half in range(2):
                            last = pe.matmul(acc(tb, half), hidden[:, t, tb * P:(tb + 1) * P],
                                             down[:, t, half * BANK:(half + 1) * BANK], start=False, stop=False,
                                             skip_group_check=True)
                last.then_inc(group_used, 1)

            with pe.Fori(0, loops) as it:
                for s in range(slots):
                    group(s, 16 * (weights.base[s] + 1) + it * 16, (it * slots + s) * 2)
            for g in range(loops * slots, total):
                group(g % slots, 16 * (weights.base[g % slots] + g // slots + 1), 2 * g)

        @ph.block.scalar
        def _(act):
            with act.Fori(0, total) as g:
                for t in range(2):
                    act.wait_ge(tile_ready, g * 2 + t + 1)
                    act.activation(silu[:, t, :], prog.psum[:, t, 0:S], ACT.Silu).then_inc(silu_ready, 1)

        @ph.block.vector
        def _(dve):
            with dve.Fori(0, total) as g:
                for t in range(2):
                    dve.wait_ge(silu_ready, g * 2 + t + 1)
                    dve.tensor_tensor(hidden[:, t, :], silu[:, t, :], prog.psum[:, t, S:2 * S], ALU.mult)\
                       .then_inc(hidden_ready, 1)
            dve.wait_ge(group_used, total)
            for tb in range(TB):
                for half in range(2):
                    at = prog.x[:, tb, half * BANK:(half + 1) * BANK]
                    dve.scalar_tensor_tensor(at, acc(tb, half), factor, at, ALU.mult, ALU.add)


def zeros_wide(prog):
    z = prog.const("zero")
    return z.bitcast(BF16).unsqueeze(1).to_broadcast([P, 2, 2 * P])


def group_stream(prog, stream, first, total):
    w = Weights(prog, [stream[first + g] for g in range(total)], 3, 3 * UNIT)
    w.stream, w.first = stream, first
    return w


def project(prog, weights, widths, lhsT, empty, kt=KT):
    starts = np.cumsum([0] + list(widths))
    with prog.phase() as ph:
        bank_full = ph.semaphore("bank_full")
        emptied = [ph.semaphore("emptied_by_scalar"), ph.semaphore("emptied_by_vector")]

        @ph.block.sync
        def _(sp):
            weights.rest(sp, bank_full, TB)

        @ph.block.tensor
        def _(pe):
            for c, n in enumerate(widths):
                weights.wait(pe, c)
                w = weights.buffer(c).rearrange("p (k n) -> p k n", k=kt)
                for tb in range(TB):
                    if c >= 4:
                        pe.wait_ge(emptied[tb], c - 3)
                    for k in range(kt):
                        last = pe.matmul(prog.psum[:, (2 * c + tb) % 8, 0:n], lhsT[:, k, tb * P:(tb + 1) * P],
                                         w[:, k, :], start=(k == 0), stop=(k == kt - 1))
                    last.then_inc(bank_full, 1)

        def take(eng, tb):
            prog.wait_small(eng)
            for c, n in enumerate(widths):
                eng.wait_ge(bank_full, 2 * c + tb + 1)
                empty(eng, prog.psum[:, (2 * c + tb) % 8, 0:n], tb, int(starts[c]), n).then_inc(emptied[tb], 1)

        @ph.block.scalar
        def _(act):
            take(act, 0)

        @ph.block.vector
        def _(dve):
            take(dve, 1)


def copy_to(z):
    def empty(eng, psum, tb, at, n):
        out = z[:, tb, at:at + n]
        if tb == 0:
            return eng.activation(out, psum, ACT.Copy)
        return eng.tensor_copy(out, psum)
    return empty


def add_projection(prog, weights, lhsT):
    with prog.phase() as ph:
        bank_full = ph.semaphore("bank_full")

        @ph.block.tensor
        def _(pe):
            for c in range(2):
                weights.wait(pe, c)
                w = weights.buffer(c).rearrange("p (k n) -> p k n", k=KT)
                for tb in range(TB):
                    for k in range(KT):
                        last = pe.matmul(prog.psum[:, 2 * c + tb, :], lhsT[:, k, tb * P:(tb + 1) * P],
                                         w[:, k, :], start=(k == 0), stop=(k == KT - 1))
                    last.then_inc(bank_full, 1)

        @ph.block.vector
        def _(dve):
            for c in range(2):
                for tb in range(TB):
                    dve.wait_ge(bank_full, 2 * c + tb + 1)
                    at = prog.x[:, tb, c * BANK:(c + 1) * BANK]
                    dve.tensor_tensor(at, prog.psum[:, 2 * c + tb, :], at, ALU.add)


class Job:

    def __init__(self, qT, kT, values, scale, hide, out, gate=None, add=False):
        self.qT, self.kT, self.values, self.scale, self.hide = qT, kT, values, scale, hide
        self.out, self.gate, self.add = out, gate, add
        self.n = kT.shape[1]


def attention(prog, jobs, mem):
    t_sb = [mem.take(S) for _ in range(2)]
    p_sb = [mem.take(S) for _ in range(2)]
    pT_sb = [mem.take(S) for _ in range(2)]
    least, sums = mem.take(2, 1), mem.take(2, 1)
    keys = lambda j: min(j.n, P)
    psum = prog.psum
    with prog.phase() as ph:
        scores, shifted, least_ready, probs, turned, turned_copied, product, taken, inverse = (
            ph.semaphore(n) for n in ("scores", "shifted", "least_ready", "probs", "turned", "turned_copied",
                                   "product", "taken", "inverse"))

        @ph.block.tensor
        def _(pe):
            prog.wait_small(pe)

            def score(i, j):
                if i >= 2:
                    pe.wait_ge(shifted, i - 1)
                pe.matmul(psum[:, i % 2, 0:j.n], j.qT, j.kT, start=True, stop=True).then_inc(scores, 1)

            def turn(i, j):
                pe.wait_ge(probs, i + 1)
                if i >= 2:
                    pe.wait_ge(turned_copied, i - 1)
                for b in range(-(-j.n // P)):
                    last = pe.transpose(psum[0:keys(j), 2 + i % 2, b * P:(b + 1) * P],
                                        p_sb[i % 2][:, b * P:b * P + keys(j)], prog.ident)
                last.then_inc(turned, 1)

            def values(i, j):
                pe.wait_ge(turned_copied, i + 1)
                if i >= 2:
                    pe.wait_ge(taken, i - 1)
                for b, v in enumerate(j.values):
                    last = pe.matmul(psum[:, 4 + i % 2, 0:HD], pT_sb[i % 2][0:keys(j), b * P:(b + 1) * P], v,
                                     start=(b == 0), stop=(b == len(j.values) - 1))
                last.then_inc(product, 1)

            for i in range(len(jobs) + 2):
                if i < len(jobs):
                    score(i, jobs[i])
                if 1 <= i <= len(jobs):
                    turn(i - 1, jobs[i - 1])
                if i >= 2:
                    values(i - 2, jobs[i - 2])

        @ph.block.vector
        def _(dve):
            prog.wait_small(dve)

            def front(i, j):
                dve.wait_ge(scores, i + 1)
                if i >= 2:
                    dve.wait_ge(probs, i - 1)
                dve.scalar_tensor_tensor(t_sb[i % 2][:, 0:j.n], psum[:, i % 2, 0:j.n], -j.scale, j.hide,
                                         ALU.mult, ALU.add).then_inc(shifted, 1)
                dve.wait_ge(shifted, i + 1)
                dve.tensor_reduce(least[:, i % 2, :], t_sb[i % 2][:, 0:j.n], AX, ALU.min).then_inc(least_ready, 1)

            def back(i, j):
                dve.wait_ge(probs, i + 1)
                if j.gate is None:
                    dve.reciprocal(sums[:, i % 2, :], sums[:, i % 2, :]).then_inc(inverse, 1)
                    dve.wait_ge(inverse, inverted[i])
                else:
                    dve.reciprocal(sums[:, i % 2, :], sums[:, i % 2, :]).then_inc(inverse, 1)
                    dve.wait_ge(inverse, inverted[i] - 1)
                    dve.tensor_tensor(sums[:, i % 2, :], sums[:, i % 2, :], j.gate, ALU.mult).then_inc(inverse, 1)
                    dve.wait_ge(inverse, inverted[i])
                dve.wait_ge(product, i + 1)
                if j.add:
                    dve.wait_ge(taken, i)
                    dve.scalar_tensor_tensor(j.out, psum[:, 4 + i % 2, 0:HD], sums[:, i % 2, :], j.out,
                                             ALU.mult, ALU.add).then_inc(taken, 1)
                else:
                    dve.tensor_scalar(j.out, psum[:, 4 + i % 2, 0:HD], sums[:, i % 2, :], None,
                                      ALU.mult).then_inc(taken, 1)

            inverted = np.cumsum([1 if j.gate is None else 2 for j in jobs]).tolist()
            for i in range(len(jobs) + 2):
                if i < len(jobs):
                    front(i, jobs[i])
                if i >= 2:
                    back(i - 2, jobs[i - 2])

        @ph.block.scalar
        def _(act):
            def copy(i, j):
                act.wait_ge(turned, i + 1)
                if i >= 2:
                    act.wait_ge(product, i - 1)
                n = -(-j.n // P) * P
                act.activation(pT_sb[i % 2][0:keys(j), 0:n], psum[0:keys(j), 2 + i % 2, 0:n], ACT.Copy)\
                   .then_inc(turned_copied, 1)

            for i in range(len(jobs) + 1):
                if i < len(jobs):
                    j = jobs[i]
                    act.wait_ge(least_ready, i + 1)
                    if i >= 2:
                        act.wait_ge(turned, i - 1)
                        act.wait_ge(taken, i - 1)
                    act.activation(p_sb[i % 2][:, 0:j.n], t_sb[i % 2][:, 0:j.n], ACT.Exp, bias=least[:, i % 2, :],
                                   scale=-1.0, accum_out=sums[:, i % 2, :]).then_inc(probs, 1)
                if i >= 1:
                    copy(i - 1, jobs[i - 1])


def causal_jobs(prog, heads, scale):
    at = prog.const_at["zero"][0]
    hide = prog.consts[:, at:at + S]
    jobs = []
    for tb in range(TB):
        n = (tb + 1) * P
        for qT, kT, values, out, gate, add in heads:
            jobs.append(Job(qT[:, tb * P:(tb + 1) * P], kT[:, 0:n], [values(b) for b in range(tb + 1)], scale,
                            hide[:, P - tb * P:S], out(tb), None if gate is None else gate(tb), add))
    return jobs


def rope_tables(prog):
    mem = Arena(prog)
    pos_i = mem.take(2 * TB).bitcast(I32)
    pos = mem.take(2 * TB)
    n1, n2 = prog.const_at["freq"][1], prog.const_at["freq2"][1]
    n = n1 + n2
    angle, turns, r, wrapped = (mem.take(TB, n) for _ in range(4))
    prog.cos = prog.rope[:, 0:TB * n].rearrange("p (b f) -> p b f", b=TB)
    prog.sin = prog.rope[:, TB * n:2 * TB * n].rearrange("p (b f) -> p b f", b=TB)
    prog.load(pos_i, prog.inp["positions"])
    two_pi = 2 * np.pi
    magic = 1.5 * 2 ** 23
    c1 = 6.28125
    c2 = float(np.float32(two_pi - c1))
    c3 = float(np.float32(two_pi - c1 - c2))
    top = float(np.nextafter(np.float32(np.pi), np.float32(0)))

    def steps(do):
        dve = do.eng
        do(dve.tensor_copy(pos, pos_i))
        for b in range(TB):
            do(dve.tensor_scalar(angle[:, b, 0:n1], prog.const("freq"), pos[:, b:b + 1], None, ALU.mult),
               dve.tensor_scalar(angle[:, b, n1:n], prog.const("freq2"), pos[:, TB + b:TB + b + 1], None, ALU.mult))
        do(dve.tensor_scalar(turns, angle, 1.0 / two_pi, magic, ALU.mult, ALU.add))
        do(dve.tensor_scalar(turns, turns, magic, None, ALU.subtract))
        do(dve.scalar_tensor_tensor(r, turns, -c1, angle, ALU.mult, ALU.add))
        do(dve.scalar_tensor_tensor(r, turns, -c2, r, ALU.mult, ALU.add))
        do(dve.scalar_tensor_tensor(r, turns, -c3, r, ALU.mult, ALU.add))
        do(dve.tensor_scalar(angle, r, np.pi / 2, None, ALU.add))
        do(dve.tensor_scalar(wrapped, angle, float(np.pi), -two_pi, ALU.is_gt, ALU.mult))
        do(dve.tensor_tensor(angle, angle, wrapped, ALU.add))
        do(dve.tensor_scalar(angle, angle, top, -top, ALU.min, ALU.max))
        do(dve.tensor_scalar(r, r, top, -top, ALU.min, ALU.max))

    prog.solo("vector", steps)

    def sines(do):
        do(do.eng.activation(prog.cos, angle, ACT.Sin), do.eng.activation(prog.sin, r, ACT.Sin))

    prog.solo("scalar", sines)


def rotate(do, prog, v, first, half, work):
    heads = v.shape[2]
    shape = [TB, heads, half]
    cos, sin = (spread(t[:, :, first:first + half].unsqueeze(2), *shape) for t in (prog.cos, prog.sin))
    x1, x2 = v[:, :, :, 0:half], v[:, :, :, half:2 * half]
    n = TB * heads * half
    w1, w2 = (work[:, i * n:(i + 1) * n].rearrange("p (b h f) -> p b h f", b=TB, h=heads) for i in range(2))
    tt = do.eng.tensor_tensor
    do(tt(w1, x1, sin, ALU.mult), tt(w2, x2, sin, ALU.mult))
    do(tt(x1, x1, cos, ALU.mult), tt(x2, x2, cos, ALU.mult))
    do(tt(x1, x1, w2, ALU.subtract), tt(x2, x2, w1, ALU.add))


def heads_of(z, at, n, width=HD):
    return z[:, :, at:at + n * width].rearrange("p b (h d) -> p b h d", h=n)


def twice(do, dst, src):
    do(do.eng.tensor_copy(dst[:, :, :, 0, :], src), do.eng.tensor_copy(dst[:, :, :, 1, :], src))


def pair_sources(v, n_pairs):
    return [v[:, b, i * P:(i + 1) * P] for i in range(n_pairs) for b in range(TB)]


def even_mixer(prog, w_in, w_out):
    nc, inp = prog.nc, prog.inp
    NH, NG, R = 12, 3, 4
    NC = 15
    A, Q, KC, VC, KS, VS, KW, VW, GL = (0, 512, 1280, 1472, 1664, 1856, 2048, 2240, 2432)
    mem = Arena(prog)
    z = mem.take(TB, 2468)
    project(prog, w_in, EVEN_CHUNKS, prog.xT, copy_to(z))
    w_out.prefetch()
    spare = prog.ring[:, 2 * KT * BANK:]
    w1 = spare[:, 0:2 * 16 * 256].rearrange("p (x l h) -> p x l h", x=2, l=16)
    w2k = spare[:, 8192:8448].rearrange("p (t d) -> p t d", t=2)
    w2v = spare[:, 8448:8576].rearrange("p (t d) -> p t d", t=2)
    wT = spare[:, 8576:9088].rearrange("p (g t) -> p g t", g=4)
    sgu_gain = spare[:, 9088:9344]
    prog.load(wT, inp["sgu_wT"].rearrange("p (g t) -> p g t", g=4))
    prog.load_row(sgu_gain, "sgu_norm")
    prog.load(w1.rearrange("p x l h -> p (x l h)"), inp["cmp_w1"])
    prog.load(spare[:, 8192:8576], inp["cmp_w2"])

    o = mem.take(TB, D)
    q_rot = mem.take(TB, NH * HD)
    dup = mem.take(4, TB, NG * 2 * HD)
    work = mem.take(2 * TB * NH * 8)
    scale, gates = mem.take(TB), mem.take(TB, 36)
    with prog.phase() as ph:
        gelu_done, gated, squared = ph.semaphore("gelu_done"), ph.semaphore("gated"), ph.semaphore("squared")
        rot = ph.semaphore("rotated")

        @ph.block.scalar
        def _(act):
            act.activation(z[:, :, A:A + 512], z[:, :, A:A + 512], ACT.Gelu_apprx_tanh).then_inc(gelu_done, 1)
            act.activation(gates, z[:, :, GL:GL + 36], ACT.Sigmoid).then_inc(gated, 1)

        @ph.block.vector
        def _(dve):
            do = Steps(dve, rot)
            do(dve.tensor_copy(q_rot, z[:, :, Q:Q + NH * HD]))
            rotate(do, prog, heads_of(q_rot, 0, NH), 0, 8, work)
            rotate(do, prog, heads_of(z, KS, NG), 0, 8, work)
            rotate(do, prog, heads_of(z, KW, NG), 0, 8, work)
            for i, at in enumerate((KC, VC, KS, KW)):
                twice(do, dup[:, i, :, :].rearrange("p b (g c d) -> p b g c d", g=NG, c=2), heads_of(z, at, NG))
            dve.wait_ge(gated, 1)
            for b in range(TB):
                cg = gates[:, b, :].rearrange("p (h n) -> p h n", n=3)[:, :, 0]
                do(dve.tensor_scalar(cg, cg, prog.const("cmp_any")[:, b:b + 1], None, ALU.mult))
    row_scales(prog, z[:, :, A + 256:A + 512], 256, scale, o[:, :, 0:256])

    def gmlp_in(do):
        dve = do.eng
        for b in range(TB):
            v = z[:, b, A + 256:A + 512]
            do(dve.scalar_tensor_tensor(v, v, scale[:, b:b + 1], sgu_gain, ALU.mult, ALU.mult))
        do(dve.tensor_tensor(wT, wT, spread(prog.const("incl").unsqueeze(1), 4, P), ALU.mult))

    prog.solo("vector", gmlp_in)
    with prog.phase() as ph:
        mixed, done = ph.semaphore("mixed"), ph.semaphore("done")

        @ph.block.tensor
        def _(pe):
            for b in range(TB):
                for g in range(4):
                    last = pe.matmul(prog.psum[:, b, g * HD:(g + 1) * HD], wT[:, g, :],
                                     z[:, b, A + 256 + g * HD:A + 256 + (g + 1) * HD], start=True, stop=True)
                last.then_inc(mixed, 1)

        @ph.block.vector
        def _(dve):
            for b in range(TB):
                dve.wait_ge(mixed, b + 1)
                for g in range(4):
                    c = slice(g * HD, (g + 1) * HD)
                    dve.scalar_tensor_tensor(o[:, b, c], prog.psum[:, b, c], prog.col("sgu_b")[:, g:g + 1],
                                             z[:, b, A + g * HD:A + (g + 1) * HD], ALU.add, ALU.mult)\
                       .then_inc(done, 1)

    qT, qrT = mem.take(NH // 2, S), mem.take(NH // 2, S)
    dupT = mem.take(4 * NG, S)
    flat = lambda v: v.rearrange("p a b -> p (a b)")
    transposes(prog, pair_sources(z[:, :, Q:Q + NH * HD], NH // 2), flat(qT))
    transposes(prog, pair_sources(q_rot, NH // 2), flat(qrT))
    transposes(prog, [dup[:, i, b, g * P:(g + 1) * P] for i in range(4) for g in range(NG) for b in range(TB)],
               flat(dupT))

    mem2 = Arena(prog, mem.at)
    blocks = mem2.take(2, 16, NG * NC)
    hidden = mem2.take(2, 2, NG * NC)
    k_cmp, v_cmp = mem2.take(NG * NC), mem2.take(NG, HD)

    def gather(do):
        dve = do.eng
        for x, name in enumerate(("cmp_pos_k", "cmp_pos_v")):
            for par in range(2):
                half = slice(par * HD, (par + 1) * HD)
                for g in range(NG):
                    t = dupT[half, NG * x + g, :].rearrange("p (n m) -> p n m", m=16)
                    src = t[:, :, par::2]
                    pos = prog.col(name)[half, :]
                    for hi in range(2):
                        do(dve.tensor_tensor(
                            blocks[half, x, 8 * hi:8 * hi + 8, g * NC:(g + 1) * NC],
                            src[:, hi:hi + NC, :].rearrange("p n l -> p l n"),
                            spread(pos[:, 8 * hi:8 * hi + 8].unsqueeze(2), 8, NC), ALU.add))

    prog.solo("vector", gather)
    with prog.phase() as ph:
        summed, hid, made, copied = (ph.semaphore(n) for n in ("summed", "hidden_done", "made", "copied"))

        @ph.block.tensor
        def _(pe):
            for x in range(2):
                for t in range(2):
                    for l in range(16):
                        last = pe.matmul(prog.psum[:, 2 * x + t, 0:NG * NC], w1[:, x, l, t * P:(t + 1) * P],
                                         blocks[:, x, l, :], start=(l == 0), stop=(l == 15))
                    last.then_inc(summed, 1)
            pe.wait_ge(hid, 4)
            for t in range(2):
                last = pe.matmul(prog.psum[:, 4, 0:NG * NC], w2k[:, t, :], hidden[:, 0, t, :], start=(t == 0),
                                 stop=(t == 1))
            for g in range(NG):
                for t in range(2):
                    last = pe.matmul(prog.psum[0:NC, 5, g * HD:(g + 1) * HD], hidden[:, 1, t, g * NC:(g + 1) * NC],
                                     w2v[:, t, :], start=(t == 0), stop=(t == 1))
            last.then_inc(made, 1)

        @ph.block.scalar
        def _(act):
            for n in range(4):
                act.wait_ge(summed, n + 1)
                act.activation(hidden[:, n // 2, n % 2, :], prog.psum[:, n, 0:NG * NC], ACT.Gelu_apprx_tanh)\
                   .then_inc(hid, 1)

        @ph.block.vector
        def _(dve):
            dve.wait_ge(made, 1)
            dve.tensor_copy(k_cmp, prog.psum[:, 4, 0:NG * NC]).then_inc(copied, 1)
            dve.tensor_copy(v_cmp[0:NC], prog.psum[0:NC, 5, 0:NG * HD].rearrange("p (g d) -> p g d", g=NG))\
               .then_inc(copied, 1)

    scale_q = HD ** -0.5
    at = prog.const_at["zero"][0]
    hide = prog.consts[:, at:at + S]
    jobs = []
    for b in range(TB):
        for h in range(NH):
            g, half = h // R, slice(h % 2 * HD, h % 2 * HD + HD)
            rows, n = slice(b * P, (b + 1) * P), (b + 1) * P
            out = o[:, b, 256 + h * HD:256 + (h + 1) * HD]
            gate = lambda i: gates[:, b, 3 * h + i:3 * h + i + 1]
            jobs.append(Job(qT[half, h // 2, rows], k_cmp[half, g * NC:(g + 1) * NC], [v_cmp[0:NC, g, :]], scale_q,
                            prog.const("cmp_hide")[:, b * NC:(b + 1) * NC], out, gate(0)))
            for i, (kt, v) in enumerate(((2, VS), (3, VW))):
                jobs.append(Job(qrT[half, h // 2, rows], dupT[half, NG * kt + g, 0:n],
                                [z[:, c, v + g * HD:v + (g + 1) * HD] for c in range(b + 1)], scale_q,
                                hide[:, P - b * P:S], out, gate(1 + i), add=True))
    attention(prog, jobs, Arena(prog, mem2.at))
    oT = Arena(prog).take(KT, S)
    transposes(prog, [o[:, b, k * P:(k + 1) * P] for k in range(KT) for b in range(TB)], flat(oT))
    add_projection(prog, w_out, oT)





def odd_mixer(prog, w_in, w_out):
    NH, NI, ID, TOP = 8, 4, 32, 64
    QC, KC, VC, QI, KI, WI, QD, KD, VD = (0, 512, 576, 640, 768, 800, 804, 1316, 1828)
    mem = Arena(prog)
    z = mem.take(TB, 2340)
    project(prog, w_in, ODD_CHUNKS, prog.xT, copy_to(z))
    w_out.prefetch()
    o = mem.take(TB, D)
    work = mem.take(2 * TB * NH * 8)
    kc2, ki4 = mem.take(TB, 1, 2, HD), mem.take(TB, NI, ID)

    def rotations(do):
        for at, n in ((QC, NH), (KC, 1), (QD, NH), (KD, NH)):
            rotate(do, prog, heads_of(z, at, n), 0, 8, work)
        rotate(do, prog, heads_of(z, QI, NI, ID), 8, 4, work)
        rotate(do, prog, heads_of(z, KI, 1, ID), 8, 4, work)
        twice(do, kc2, heads_of(z, KC, 1))
        for i in range(NI):
            do(do.eng.tensor_copy(ki4[:, :, i, :], z[:, :, KI:KI + ID]))

    prog.solo("vector", rotations)
    turned = mem.take(4 + 4 + 4 + 3, S)
    flat = lambda v: v.rearrange("p a b -> p (a b)")
    qcT, qdT, kdT, rest = turned[:, 0:4], turned[:, 4:8], turned[:, 8:12], turned[:, 12:15]
    transposes(prog, [t for at in (QC, QD, KD) for t in pair_sources(z[:, :, at:at + 512], 4)] +
               pair_sources(kc2.rearrange("p b h c d -> p b (h c d)"), 1) +
               pair_sources(z[:, :, QI:QI + P], 1) + pair_sources(ki4.rearrange("p b h d -> p b (h d)"), 1), flat(turned))
    kcT, qiT, kiT = (rest[:, i, :] for i in range(3))

    relu, score, picked = mem.take(NI, S), mem.take(TB, S), mem.take(TB, S)
    top, hide_all = mem.take(8), mem.take(TB, S)
    at = prog.const_at["zero"][0]
    hide = lambda b: prog.consts[:, at + P - b * P:at + S]
    scored = NI
    with prog.phase() as ph:
        logits, rectified, done = ph.semaphore("logits"), ph.semaphore("rectified"), ph.semaphore("done")

        @ph.block.tensor
        def _(pe):
            for b in range(TB):
                for h in range(NI):
                    rows = slice(h * ID, (h + 1) * ID)
                    last = pe.matmul(prog.psum[:, b * NI + h, 0:(b + 1) * P], qiT[rows, b * P:(b + 1) * P],
                                     kiT[rows, 0:(b + 1) * P], start=True, stop=True)
                last.then_inc(logits, 1)

        @ph.block.scalar
        def _(act):
            for b in range(TB):
                n = (b + 1) * P
                act.wait_ge(logits, b + 1)
                if b:
                    act.wait_ge(done, scored)
                act.activation(relu[:, :, 0:n], prog.psum[:, b * NI:(b + 1) * NI, 0:n], ACT.Relu,
                               scale=float(ID ** -0.5)).then_inc(rectified, 1)

        @ph.block.vector
        def _(dve):
            do = Steps(dve, done)
            for b in range(TB):
                n = (b + 1) * P
                dve.wait_ge(rectified, b + 1)
                for h in range(NI):
                    w = z[:, b, WI + h:WI + h + 1]
                    if h == 0:
                        do(dve.tensor_scalar(score[:, b, 0:n], relu[:, h, 0:n], w, None, ALU.mult))
                    else:
                        do(dve.scalar_tensor_tensor(score[:, b, 0:n], relu[:, h, 0:n], w, score[:, b, 0:n],
                                                    ALU.mult, ALU.add))
                do(dve.scalar_tensor_tensor(score[:, b, 0:n], score[:, b, 0:n], NI ** -0.5, hide(b), ALU.mult,
                                            ALU.subtract))
                src = score[:, b, 0:n]
                for r in range(TOP // 8):
                    do(dve.max(top, src))
                    do(dve.match_replace(picked[:, b, 0:n], top, src, -3e38))
                    src = picked[:, b, 0:n]
                do(dve.tensor_scalar(picked[:, b, 0:n], src, -2e38, -BIG, ALU.is_lt, ALU.mult))
                do(dve.tensor_scalar(picked[:, b, 0:n], src, BIG, None, ALU.add))
                do(dve.tensor_tensor(hide_all[:, b, 0:n], picked[:, b, 0:n], hide(b), ALU.add))

    scale_q = HD ** -0.5
    jobs = []
    for b in range(TB):
        rows, n = slice(b * P, (b + 1) * P), (b + 1) * P
        for h in range(NH):
            half = slice(h % 2 * HD, h % 2 * HD + HD)
            jobs.append(Job(qcT[half, h // 2, rows], kcT[half, 0:n], [z[:, c, VC:VC + HD] for c in range(b + 1)],
                            scale_q, hide_all[:, b, 0:n], o[:, b, h * HD:(h + 1) * HD]))
        for h in range(NH):
            half = slice(h % 2 * HD, h % 2 * HD + HD)
            jobs.append(Job(qdT[half, h // 2, rows], kdT[half, h // 2, 0:n],
                            [z[:, c, VD + h * HD:VD + (h + 1) * HD] for c in range(b + 1)],
                            scale_q, hide(b), o[:, b, 512 + h * HD:512 + (h + 1) * HD]))
    attention(prog, jobs, Arena(prog, mem.at))
    oT = Arena(prog).take(KT, S)
    transposes(prog, [o[:, b, k * P:(k + 1) * P] for k in range(KT) for b in range(TB)], flat(oT))
    add_projection(prog, w_out, oT)


def final_norm(prog):
    mem = Arena(prog)
    work, scale, gain = mem.take(TB, D), mem.take(TB), mem.take(D)
    prog.load_row(gain, "final_norm")
    row_scales(prog, prog.x, D, scale, work)

    def steps(do):
        for b in range(TB):
            do(do.eng.scalar_tensor_tensor(prog.x[:, b, :], prog.x[:, b, :], scale[:, b:b + 1], gain, ALU.mult, ALU.mult))

    prog.solo("vector", steps)


NH8 = 8
PAIRS = NH8 // 2


def by_parity(psum, bank, h):
    return psum[:, bank + 4 * (h % 2), h // 2 * HD:(h // 2 + 1) * HD]


def both_parities(psum, bank):
    return psum[:, bank:bank + 5:4, 0:PAIRS * HD].rearrange("p x (i d) -> p i x d", i=PAIRS)


def paired(v):
    return v.rearrange("p (i x) d -> p i x d", x=2)


def invert(prog, below, full, full_T, level_part, product):
    at = prog.const_at["level0"][0]
    level = lambda l: prog.consts[:, at + l * P:at + (l + 1) * P]
    group = lambda v, g: v[:, 4 * g:4 * g + 4, :]
    last_level = 6

    def start(do):
        for g in range(2):
            do(do.eng.tensor_tensor(group(full_T, g), group(below, g), spread(level(0).unsqueeze(1), 4, P), ALU.mult))
            do(do.eng.tensor_tensor(group(full_T, g), group(full_T, g), spread(prog.ident.unsqueeze(1), 4, P), ALU.add))

    prog.solo("vector", start)
    transposes(prog, [full_T[:, h, :] for h in range(NH8)], full.rearrange("p h t -> p (h t)"))
    with prog.phase() as ph:
        part_ready, first, first_copied, second, joined = (
            ph.semaphore(n) for n in ("part_ready", "first_product", "first_copied", "second_product", "joined"))
        order = [(l, g) for l in range(1, last_level + 1) for g in range(2)]
        bank = lambda kind, g: prog.psum[:, kind * 2 + g, :]

        @ph.block.gpsimd
        def _(pool):
            for n, (l, g) in enumerate(order):
                if n >= 2:
                    pool.wait_ge(first, n - 1)
                pool.tensor_tensor(group(level_part, g), group(below, g), spread(level(l).unsqueeze(1), 4, P),
                                   ALU.mult).then_inc(part_ready, 1)

        @ph.block.tensor
        def _(pe):
            def products_one(n):
                l, g = order[n]
                pe.wait_ge(part_ready, n + 1)
                if n >= 2:
                    pe.wait_ge(joined, 2 * (n - 1))
                for h in range(4):
                    last = pe.matmul(bank(0, g)[:, h * P:(h + 1) * P], level_part[:, 4 * g + h, :],
                                     full[:, 4 * g + h, :], start=True, stop=True)
                last.then_inc(first, 1)

            def products_two(n):
                l, g = order[n]
                pe.wait_ge(first_copied, n + 1)
                for h in range(4):
                    y = product[:, 4 * g + h, :]
                    last = pe.matmul(bank(2, g)[:, h * P:(h + 1) * P], y, full_T[:, 4 * g + h, :], start=True, stop=True)
                last.then_inc(second, 1)
                for h in range(4):
                    y = product[:, 4 * g + h, :]
                    last = pe.matmul(bank(1, g)[:, h * P:(h + 1) * P], full_T[:, 4 * g + h, :], y, start=True, stop=True)
                last.then_inc(second, 1)

            for n in range(0, len(order), 2):
                products_one(n)
                products_one(n + 1)
                products_two(n)
                products_two(n + 1)

        @ph.block.scalar
        def _(act):
            for n, (l, g) in enumerate(order):
                act.wait_ge(first, n + 1)
                if n >= 2:
                    act.wait_ge(second, 2 * (n - 1))
                act.activation(group(product, g), bank(0, g).rearrange("p (h t) -> p h t", h=4), ACT.Copy)\
                   .then_inc(first_copied, 1)

        @ph.block.vector
        def _(dve):
            for n, (l, g) in enumerate(order):
                dve.wait_ge(second, 2 * (n + 1))
                for kind, x in ((2, full_T), (1, full)):
                    dve.tensor_tensor(group(x, g), group(x, g), bank(kind, g).rearrange("p (h t) -> p h t", h=4),
                                      ALU.add).then_inc(joined, 1)


def head_sums_scale(prog, v, n_tiles, eps, factor, squares, scale):
    with prog.phase() as ph:
        squared, summed, rooted, ready = (ph.semaphore(n) for n in ("squared", "summed", "rooted", "ready"))

        @ph.block.scalar
        def _(act):
            act.activation(squares, v, ACT.Square).then_inc(squared, 1)
            act.wait_ge(ready, 1)
            act.activation(scale, scale, ACT.Sqrt).then_inc(rooted, 1)

        @ph.block.tensor
        def _(pe):
            pe.wait_ge(squared, 1)
            for i in range(n_tiles):
                last = pe.matmul(prog.psum[:, i // 2, i % 2 * S:(i % 2 + 1) * S], prog.const("head_ones"),
                                 squares[:, i, :], start=True, stop=True)
            last.then_inc(summed, 1)

        @ph.block.vector
        def _(dve):
            dve.wait_ge(summed, 1)
            dve.tensor_scalar(scale, prog.psum[:, 0:n_tiles // 2, :].rearrange("p b (i t) -> p (b i) t", t=S),
                              eps, None, ALU.add).then_inc(ready, 1)
            dve.wait_ge(rooted, 1)
            dve.reciprocal(scale, scale).then_inc(ready, 1)
            if factor != 1.0:
                dve.wait_ge(ready, 2)
                dve.tensor_scalar(scale, scale, factor, None, ALU.mult).then_inc(ready, 1)


def rwkv_branch(prog, layer, zT, o, v_first, ring):
    inp, psum = prog.inp, prog.psum
    col = lambda name: prog.col(f"{name}{layer}")
    mem = Arena(prog, ring)
    take, flat = mem.take, lambda v: v.rearrange("p a b -> p (a b)")
    spare = RingMemory(prog)
    lora = spare.take(2 * BANK)
    prog.load(lora, inp[f"lora_up{layer}"])
    if layer:
        vres_down, vres_up = spare.take(KT, 32), spare.take(BANK)
        prog.load(flat(vres_down), inp["vres_down"])
        prog.load(vres_up[0:32], inp["vres_up"])
    gate = spare.take(TB, BANK)
    bonus = take(TB, NH8)
    r, k, v = zT[:, 0:4], zT[:, 4:8], zT[:, 8:12]
    t4 = lambda c, n=4: spread(c.unsqueeze(2), n, S)

    mark = spare.at
    diff = spare.take(14, S)

    def shift(do):
        dve = do.eng
        z = zT[:, 0:14]
        do(dve.tensor_tensor(diff[:, :, 1:S], z[:, :, 0:S - 1], z[:, :, 1:S], ALU.subtract),
           dve.tensor_scalar(diff[:, :, 0:1], z[:, :, 0:1], -1.0, None, ALU.mult))
        do(dve.tensor_tensor(diff, diff, t4(col("rwkv_mu_2"), 14), ALU.mult))
        do(dve.tensor_tensor(z, z, diff, ALU.add))

    prog.solo("vector", shift)
    spare.at = mark
    decay, rate = spare.take(4, S), spare.take(4, S)
    xv = spare.take(KT, S) if layer else None
    xv_low = spare.take(S) if layer else None
    mix = spare.take(4, S) if layer else None
    with prog.phase() as ph:
        squashed, made, taken, mixed, low, low_copied = (
            ph.semaphore(n) for n in ("squashed", "made", "taken", "mixed", "low", "low_copied"))

        @ph.block.scalar
        def _(act):
            act.activation(zT[0:HD, 12, :], zT[0:HD, 12, :], ACT.Tanh).then_inc(squashed, 1)
            act.activation(zT[:, 13, :], zT[:, 13, :], ACT.Sigmoid).then_inc(squashed, 1)
            act.wait_ge(made, 1)
            for i in range(4):
                act.activation(decay[:, i, :], psum[:, i // 2, i % 2 * S:(i % 2 + 1) * S], ACT.Sigmoid,
                               bias=col("rwkv_w0_2")[:, i:i + 1]).then_inc(taken, 1)
                act.activation(rate[:, i, :], psum[:, 2 + i // 2, i % 2 * S:(i % 2 + 1) * S], ACT.Sigmoid,
                               bias=col("rwkv_a0_2")[:, i:i + 1]).then_inc(taken, 1)
            if layer:
                act.wait_ge(made, 2)
                for i in range(4):
                    act.activation(mix[:, i, :], psum[:, 6 + i // 2, i % 2 * S:(i % 2 + 1) * S], ACT.Sigmoid,
                                   bias=prog.col("vres_b_2")[:, i:i + 1]).then_inc(taken, 1)

        @ph.block.tensor
        def _(pe):
            prog.wait_small(pe)
            pe.wait_ge(squashed, 2)
            for i in range(4):
                c = slice(i * P, (i + 1) * P)
                pe.matmul(psum[:, i // 2, i % 2 * S:(i % 2 + 1) * S], lora[0:HD, c], zT[0:HD, 12, :], start=True, stop=True)
            for i in range(4):
                c = slice(i * P, (i + 1) * P)
                pe.matmul(psum[:, 2 + i // 2, i % 2 * S:(i % 2 + 1) * S], lora[HD:P, c], zT[HD:P, 12, :], start=True, stop=True)
            for b in range(TB):
                last = pe.matmul(psum[:, 4 + b, :], zT[:, 13, b * P:(b + 1) * P], lora[:, BANK:2 * BANK], start=True, stop=True)
            last.then_inc(made, 1)
            if layer:
                pe.wait_ge(mixed, 4)
                pe.wait_ge(taken, 8)
                for i in range(KT):
                    last = pe.matmul(psum[0:32, 0, 0:S], vres_down[:, i, :], xv[:, i, :], start=(i == 0), stop=(i == KT - 1))
                last.then_inc(low, 1)
                pe.wait_ge(low_copied, 1)
                for i in range(4):
                    last = pe.matmul(psum[:, 6 + i // 2, i % 2 * S:(i % 2 + 1) * S], vres_up[0:32, i * P:(i + 1) * P],
                                     xv_low[0:32], start=True, stop=True)
                last.then_inc(made, 1)

        @ph.block.vector
        def _(dve):
            if layer:
                do = Steps(dve, mixed)
                u = prog.xT
                do(dve.tensor_tensor(xv[:, :, 1:S], u[:, :, 0:S - 1], u[:, :, 1:S], ALU.subtract),
                   dve.tensor_scalar(xv[:, :, 0:1], u[:, :, 0:1], -1.0, None, ALU.mult))
                do(dve.tensor_tensor(xv, xv, t4(prog.col("vres_mu_2"), KT), ALU.mult))
                do(dve.tensor_tensor(xv, xv, u, ALU.add))
                dve.wait_ge(low, 1)
                dve.tensor_copy(xv_low[0:32], psum[0:32, 0, 0:S]).then_inc(low_copied, 1)
            dve.wait_ge(made, 1)
            for b in range(TB):
                dve.tensor_copy(gate[:, b, :], psum[:, 4 + b, :]).then_inc(mixed, 1)

    if layer:
        def value_mix(do):
            tt = do.eng.tensor_tensor
            do(tt(xv[:, 0:4], v_first, v, ALU.subtract))
            do(tt(xv[:, 0:4], xv[:, 0:4], mix, ALU.mult))
            do(tt(v, v, xv[:, 0:4], ALU.add))

        prog.solo("vector", value_mix)
    else:
        prog.solo("vector", lambda do: do(do.eng.tensor_copy(v_first, v)))
    if layer:
        spare.at = mark + 2 * 4 * S

    kk, scale, products = spare.take(4, S), spare.take(4, S), spare.take(4, S)
    prog.solo("vector", lambda do: do(do.eng.tensor_tensor(kk, k, t4(col("rwkv_k_k_2")), ALU.mult)))
    head_sums_scale(prog, kk, 4, 1e-12, 1.0, products, scale)

    log_w = decay
    run, middle = scale, take(PAIRS, TB, 1)
    first_scale, join_scale = take(PAIRS, TB), take(PAIRS)

    def keys(do):
        dve = do.eng
        do(dve.tensor_tensor(kk, kk, scale, ALU.mult), dve.tensor_scalar(log_w, decay, float(-np.exp(-0.5)), None, ALU.mult))
        do(dve.scalar_tensor_tensor(products, rate, 1.0, t4(col("rwkv_k_a_2")), ALU.subtract, ALU.mult))
        do(dve.scalar_tensor_tensor(k, products, 1.0, k, ALU.add, ALU.mult))
        do(dve.tensor_tensor(products, r, k, ALU.mult), dve.tensor_tensor(rate, rate, kk, ALU.mult))
        do(dve.tensor_tensor(products, products, t4(col("rwkv_r_k_2")), ALU.mult))
        for i in range(PAIRS):
            for c in range(TB):
                t = slice(c * P, (c + 1) * P)
                do(dve.tensor_tensor_scan(run[:, i, t], prog.const("ones"), log_w[:, i, t], 0.0, ALU.mult, ALU.add))
        m = run.rearrange("p i (c t) -> p i c t", c=TB)
        do(dve.tensor_scalar(middle, m[:, :, :, P // 2 - 1:P // 2], -1.0, None, ALU.mult))
        do(dve.tensor_tensor(join_scale, m[:, :, 0, P - 1], middle[:, :, 0, 0], ALU.add))
        do(dve.tensor_tensor(join_scale, join_scale, middle[:, :, 1, 0], ALU.subtract))
        do(dve.tensor_tensor(m, m, spread(middle, PAIRS, TB, P), ALU.add))

    prog.solo("vector", keys)
    grown, shrunk = spare.take(4, S), take(4, S)
    ra = spare.take(PAIRS, TB, 2, P)
    bk = spare.take(2, PAIRS, S)

    def exponentials(do):
        act = do.eng
        do(act.activation(grown, run, ACT.Exp), act.activation(shrunk, run, ACT.Exp, scale=-1.0),
           act.activation(first_scale, middle.rearrange("p i c o -> p i (c o)"), ACT.Exp),
           act.activation(join_scale, join_scale, ACT.Exp))

    prog.solo("scalar", exponentials)

    def scaled(do):
        dve = do.eng
        c4 = lambda x: x.rearrange("p i (c t) -> p i c t", c=TB)
        g, kkc = c4(grown), c4(kk)
        do(dve.tensor_tensor(ra[:, :, :, 0, :], c4(r), g, ALU.mult),
           dve.tensor_tensor(bk[:, 0], rate, shrunk, ALU.mult),
           dve.tensor_tensor(bk[:, 1], k, shrunk, ALU.mult))
        for c in range(TB):
            do(dve.scalar_tensor_tensor(ra[:, :, c, 1, 1:P], kkc[:, :, c, 1:P], -1.0, g[:, :, c, 0:P - 1], ALU.mult, ALU.mult),
               dve.scalar_tensor_tensor(ra[:, :, c, 1, 0:1], kkc[:, :, c, 0:1], -1.0, first_scale[:, :, c:c + 1], ALU.mult, ALU.mult))

    prog.solo("vector", scaled)
    with prog.phase() as ph:
        summed = ph.semaphore("summed")

        @ph.block.tensor
        def _(pe):
            for b in range(TB):
                for i in range(PAIRS):
                    last = pe.matmul(psum[:, b, 2 * i:2 * i + 2], products[:, i, b * P:(b + 1) * P],
                                     prog.const("head_pick"), start=True, stop=True)
            last.then_inc(summed, 1)

        @ph.block.vector
        def _(dve):
            dve.wait_ge(summed, 1)
            dve.tensor_copy(bonus, psum[:, 0:2, 0:NH8]).then_inc(summed, 1)

    token_major = spare.take(3, TB, BANK)
    transposes(prog, [src[:, i, b * P:(b + 1) * P] for src in (v, bk[:, 0], bk[:, 1]) for b in range(TB)
                      for i in range(PAIRS)], token_major.rearrange("p w b n -> p (w b n)"))
    v_tok, b_tok, k_tok = (token_major[:, i] for i in range(3))

    state = take(PAIRS, HD)
    rhs, u = take(NH8, HD), take(NH8, HD)
    masks_at = prog.const_at["incl"][0]
    masks = prog.consts[:, masks_at:masks_at + 2 * P]
    mem3 = Arena(prog, mem.at)
    m = Free(prog, mem3, spare)
    scores = m.take(NH8, 2, 2, P)
    full, full_T, part, product = m.take(NH8, P), m.take(NH8, P), m.take(NH8, P), m.take(NH8, P)
    y = o[:, :, 0:BANK]
    for c in range(TB):
        with prog.phase() as ph:
            scored, masked = ph.semaphore("scored"), ph.semaphore("masked")

            @ph.block.tensor
            def _(pe):
                for h in range(NH8):
                    half = slice(h % 2 * HD, h % 2 * HD + HD)
                    for w in range(2):
                        last = pe.matmul(psum[:, h, w * S:(w + 1) * S], bk[half, w, h // 2, c * P:(c + 1) * P],
                                         ra[half, h // 2, c].rearrange("p x t -> p (x t)"), start=True, stop=True)
                    last.then_inc(scored, 1)

            @ph.block.vector
            def _(dve):
                for h in range(NH8):
                    dve.wait_ge(scored, h + 1)
                    dve.tensor_tensor(scores[:, h].rearrange("p w x t -> p w (x t)"),
                                      psum[:, h, :].rearrange("p (w n) -> p w n", w=2),
                                      spread(masks.unsqueeze(1), 2, 2 * P), ALU.mult).then_inc(masked, 1)
        invert(prog, scores[:, :, 0, 1, :], full, full_T, part, product)
        with prog.phase() as ph:
            rhs_made, rhs_copied, u_made, u_copied, y_made, done = (
                ph.semaphore(n) for n in ("rhs_made", "rhs_copied", "u_made", "u_copied", "y_made", "done"))

            @ph.block.tensor
            def _(pe):
                heads = [(h, slice(h % 2 * HD, h % 2 * HD + HD), slice(h * HD, (h + 1) * HD)) for h in range(NH8)]
                for h, half, cols in heads:
                    at = by_parity(psum, 0, h)
                    last = pe.matmul(at, scores[:, h, 1, 1, :], v_tok[:, c, cols], start=True, stop=(c == 0))
                    if c:
                        last = pe.matmul(at, ra[half, h // 2, c, 1, :], state[half, h // 2, :], start=False, stop=True)
                last.then_inc(rhs_made, 1)
                pe.wait_ge(rhs_copied, 1)
                for h, half, cols in heads:
                    last = pe.matmul(psum[:, 1, cols], full_T[:, h, :], rhs[:, h, :], start=True, stop=True)
                last.then_inc(u_made, 1)
                pe.wait_ge(u_copied, 1)
                for h, half, cols in heads:
                    at = by_parity(psum, 2, h)
                    pe.matmul(at, scores[:, h, 0, 0, :], u[:, h, :], start=True, stop=False)
                    last = pe.matmul(at, scores[:, h, 1, 0, :], v_tok[:, c, cols], start=False, stop=(c == 0))
                    if c:
                        last = pe.matmul(at, ra[half, h // 2, c, 0, :], state[half, h // 2, :], start=False, stop=True)
                last.then_inc(y_made, 1)
                if c == 0:
                    for h, half, cols in heads:
                        at = psum[half, 7, h // 2 * HD:(h // 2 + 1) * HD]
                        pe.matmul(at, b_tok[:, c, cols], u[:, h, :], start=True, stop=False)
                        last = pe.matmul(at, k_tok[:, c, cols], v_tok[:, c, cols], start=False, stop=True)
                    last.then_inc(y_made, 1)

            @ph.block.vector
            def _(dve):
                dve.wait_ge(rhs_made, 1)
                dve.tensor_copy(paired(rhs), both_parities(psum, 0)).then_inc(rhs_copied, 1)
                dve.wait_ge(u_made, 1)
                dve.tensor_copy(u.rearrange("p h d -> p (h d)"), psum[:, 1, :]).then_inc(u_copied, 1)
                dve.wait_ge(y_made, 1)
                dve.tensor_copy(paired(y[:, c, :].rearrange("p (h d) -> p h d", h=NH8)), both_parities(psum, 2)).then_inc(done, 1)
                if c == 0:
                    dve.wait_ge(y_made, 2)
                    dve.tensor_tensor(state, psum[:, 7, 0:PAIRS * HD].rearrange("p (i d) -> p i d", i=PAIRS),
                                      spread(join_scale.unsqueeze(2), PAIRS, HD), ALU.mult).then_inc(done, 1)

    m = Free(prog, Arena(prog, mem.at), spare)
    gain, offset, sq = m.take(BANK), m.take(BANK), m.take(TB, NH8, HD)
    stat = m.take(TB, NH8)
    prog.load_row(gain, f"rwkv_ln_g_2{layer}")
    prog.load_row(offset, f"rwkv_ln_b_2{layer}")
    yh = y.rearrange("p b (h d) -> p b h d", h=NH8)
    per_head = lambda s: spread(s.unsqueeze(3), TB, NH8, HD)
    row = lambda g: spread(g.unsqueeze(1), TB, BANK)

    def centre(do):
        dve = do.eng
        do(dve.tensor_reduce(stat, yh, AX, ALU.add))
        do(dve.tensor_scalar(stat, stat, 1.0 / HD, None, ALU.mult))
        do(dve.tensor_tensor(yh, yh, per_head(stat), ALU.subtract))
        do(dve.tensor_tensor(sq, yh, yh, ALU.mult))
        do(dve.tensor_reduce(stat, sq, AX, ALU.add))
        do(dve.tensor_scalar(stat, stat, 1.0 / HD, 64e-5, ALU.mult, ALU.add))

    prog.solo("vector", centre)
    prog.solo("scalar", lambda do: do(do.eng.activation(stat, stat, ACT.Sqrt)))

    def finish(do):
        tt = do.eng.tensor_tensor
        do(do.eng.reciprocal(stat, stat), tt(sq, v_tok.rearrange("p b (h d) -> p b h d", h=NH8), per_head(bonus), ALU.mult))
        do(tt(yh, yh, per_head(stat), ALU.mult))
        do(tt(y, y, row(gain), ALU.mult))
        do(tt(y, y, row(offset), ALU.add))
        do(tt(yh, yh, sq, ALU.add))
        do(tt(y, y, gate, ALU.mult))

    prog.solo("vector", finish)


class RingMemory:

    def __init__(self, prog):
        self.prog, self.at = prog, 0

    def take(self, *shape):
        n = int(np.prod(shape))
        assert self.at + n <= RING, ("ring", self.at, n)
        v = self.prog.ring[:, self.at:self.at + n]
        self.at += n
        if len(shape) == 1:
            return v
        names = "abcd"[:len(shape)]
        kw = {names[i]: shape[i] for i in range(len(shape) - 1)}
        return v.rearrange(f"p ({' '.join(names)}) -> p {' '.join(names)}", **kw)


class Free:

    def __init__(self, prog, arena, ring):
        self.prog, self.arena, self.ring = prog, arena, ring

    def take(self, *shape):
        n = int(np.prod(shape))
        if self.arena.at + n <= self.prog.arena_size:
            return self.arena.take(*shape)
        return self.ring.take(*shape)


def gdn_branch(prog, layer, zT, ba, gate, o, at):
    psum, inp = prog.psum, prog.inp
    flat = lambda v: v.rearrange("p a b -> p (a b)")
    mem, spare = Arena(prog, at), RingMemory(prog)
    conv = spare.take(12, S)
    gate_s, squares = spare.take(TB, BANK), spare.take(8, S)
    scale = mem.take(8, S)
    w = prog.col(f"gdn_conv_w_2{layer}")
    a_log, dt, beta, g = mem.take(NH8), mem.take(NH8), mem.take(TB, NH8), mem.take(TB, NH8)
    sp, pos = mem.take(TB, NH8), mem.take(TB, NH8)
    gain = mem.take(HD)
    prog.load_row(a_log, f"gdn_a_log_2{layer}")
    prog.load_row(dt, f"gdn_dt_bias_2{layer}")
    prog.load_row(gain, f"gdn_norm_g_2{layer}")
    with prog.phase() as ph:
        started, added, silu_done, logit, exped, logged = (
            ph.semaphore(n) for n in ("started", "added", "silu_done", "logit", "exped", "logged"))

        @ph.block.scalar
        def _(act):
            prog.wait_small(act)
            for i in range(12):
                act.activation(conv[:, i, :], zT[:, i, :], ACT.Copy, scale=w[:, 36 + i:37 + i]).then_inc(started, 1)
            act.activation(beta, ba[:, :, 0:NH8], ACT.Sigmoid).then_inc(exped, 1)
            act.activation(a_log, a_log, ACT.Exp).then_inc(exped, 1)
            act.wait_ge(logit, 4)
            act.activation(sp, sp, ACT.Exp, scale=-1.0).then_inc(exped, 1)
            act.wait_ge(exped, 3)
            act.activation(sp, sp, ACT.Ln, bias=1.0).then_inc(logged, 1)
            for i in range(3):
                act.wait_ge(added, 36)
                act.activation(conv[:, 4 * i:4 * i + 4, :], conv[:, 4 * i:4 * i + 4, :], ACT.Silu).then_inc(silu_done, 1)
            act.activation(gate_s, gate, ACT.Silu).then_inc(silu_done, 1)

        @ph.block.vector
        def _(dve):
            prog.wait_small(dve)
            do = Steps(dve, logit)
            do(dve.tensor_tensor(pos, ba[:, :, NH8:2 * NH8], spread(dt.unsqueeze(1), TB, NH8), ALU.add))
            do(dve.tensor_scalar(sp, pos, -1.0, None, ALU.mult))
            do(dve.tensor_tensor(sp, sp, pos, ALU.max))
            do(dve.tensor_scalar(pos, pos, 0.0, None, ALU.max))
            for j in range(3):
                s = 3 - j
                for i in range(12):
                    n = j * 12 + i
                    if j == 0:
                        dve.wait_ge(started, i + 1)
                    else:
                        dve.wait_ge(added, n - 11)
                    dve.scalar_tensor_tensor(conv[:, i, s:S], zT[:, i, 0:S - s], w[:, n:n + 1], conv[:, i, s:S],
                                             ALU.mult, ALU.add).then_inc(added, 1)
            dve.wait_ge(logged, 1)
            dve.wait_ge(exped, 2)
            do(dve.tensor_tensor(g, pos, sp, ALU.add))
            do(dve.scalar_tensor_tensor(g, g, -1.0, spread(a_log.unsqueeze(1), TB, NH8), ALU.mult, ALU.mult))
    head_sums_scale(prog, conv[:, 0:8], 8, 1e-12, 1.0, squares, scale)
    qk = mem.take(PAIRS, TB, 2, P)

    def unit(do):
        c4 = lambda x: x.rearrange("p i (c t) -> p i c t", c=TB)
        do(do.eng.scalar_tensor_tensor(flat(conv[:, 0:4]), flat(conv[:, 0:4]), HD ** -0.5, flat(scale[:, 0:4]), ALU.mult, ALU.mult),
           do.eng.tensor_tensor(conv[:, 4:8], conv[:, 4:8], scale[:, 4:8], ALU.mult))
        do(do.eng.tensor_copy(qk[:, :, :, 0, :], c4(conv[:, 0:4])), do.eng.tensor_copy(qk[:, :, :, 1, :], c4(conv[:, 4:8])))

    prog.solo("vector", unit)
    spare.at -= 8 * S
    token_major = spare.take(2, TB, BANK)
    transposes(prog, [conv[:, 4 * x + i, b * P:(b + 1) * P] for x in (1, 2) for b in range(TB) for i in range(PAIRS)],
               token_major.rearrange("p w b n -> p (w b n)"))
    k_tok, v_tok = token_major[:, 0], token_major[:, 1]

    grown, left, beta_neg = mem.take(TB, NH8), mem.take(TB, NH8), mem.take(TB, NH8)
    with prog.phase() as ph:
        summed, ready, done = ph.semaphore("summed"), ph.semaphore("ready"), ph.semaphore("done")

        @ph.block.tensor
        def _(pe):
            for c in range(TB):
                pe.matmul(psum[:, 0, c * NH8:(c + 1) * NH8], prog.const("incl"), g[:, c, :], start=True, stop=True)
                last = pe.matmul(psum[:, 1, c * NH8:(c + 1) * NH8], prog.const("after"), g[:, c, :], start=True, stop=True)
            last.then_inc(summed, 1)

        @ph.block.scalar
        def _(act):
            act.wait_ge(summed, 1)
            act.activation(flat(grown), psum[:, 0, 0:TB * NH8], ACT.Exp).then_inc(ready, 1)
            act.activation(flat(left), psum[:, 1, 0:TB * NH8], ACT.Exp).then_inc(ready, 1)

        @ph.block.vector
        def _(dve):
            dve.tensor_scalar(beta_neg, beta, -1.0, None, ALU.mult).then_inc(done, 1)

    state = mem.take(PAIRS, HD)
    rhs, u, u2 = mem.take(NH8, HD), mem.take(NH8, HD), mem.take(NH8, HD)
    m = Free(prog, mem, spare)
    scores = m.take(NH8, 2, P)
    gamma = m.take(NH8, P)
    full, full_T, part, product = m.take(NH8, P), m.take(NH8, P), m.take(NH8, P), m.take(NH8, P)
    masked_gamma = m.take(2, 2, P)
    masks_at = prog.const_at["incl"][0]
    masks = prog.consts[:, masks_at:masks_at + 2 * P].rearrange("p (x t) -> p x t", x=2)
    y = o[:, :, 2 * BANK:3 * BANK]
    per_head = lambda s: spread(s.unsqueeze(2), NH8, HD)
    heads_v = lambda v: v.rearrange("p (h d) -> p h d", h=NH8)
    scored_at = lambda h: psum[:, h % 2 * 2 + h // 4, h // 2 % 2 * S:(h // 2 % 2 + 1) * S]
    for c in range(TB):
        with prog.phase() as ph:
            spread_done, gamma_sum, gamma_done, scored, masked, done = (
                ph.semaphore(n) for n in ("spread_done", "gamma_sum", "gamma_done", "scored", "masked", "done"))

            @ph.block.gpsimd
            def _(pool):
                for h in range(NH8):
                    pool.tensor_scalar(part[:, h, :], prog.const("after"), g[:, c, h:h + 1], None, ALU.mult).then_inc(spread_done, 1)

            @ph.block.tensor
            def _(pe):
                for h in range(NH8):
                    half = slice(h % 2 * HD, h % 2 * HD + HD)
                    pe.matmul(scored_at(h), qk[half, h // 2, c, 1, :],
                              qk[half, h // 2, c].rearrange("p x t -> p (x t)"), start=True, stop=True).then_inc(scored, 1)
                for h in range(NH8):
                    pe.wait_ge(spread_done, h + 1)
                    pe.matmul(psum[:, 4 + h // 4, h % 4 * P:(h % 4 + 1) * P], part[:, h, :], prog.const("incl"),
                              start=True, stop=True).then_inc(gamma_sum, 1)

            @ph.block.scalar
            def _(act):
                for b in range(2):
                    act.wait_ge(gamma_sum, 4 * (b + 1))
                    act.activation(gamma[:, 4 * b:4 * b + 4, :].rearrange("p h t -> p (h t)"), psum[:, 4 + b, :], ACT.Exp)\
                       .then_inc(gamma_done, 1)

            @ph.block.vector
            def _(dve):
                for h in range(NH8):
                    dve.wait_ge(gamma_done, h // 4 + 1)
                    dve.wait_ge(scored, h + 1)
                    if h >= 2:
                        dve.wait_ge(done, 2 * (h - 1))
                    mg = masked_gamma[:, h % 2]
                    dve.tensor_tensor(mg, spread(gamma[:, h, :].unsqueeze(1), 2, P), masks, ALU.mult).then_inc(masked, 1)
                    dve.wait_ge(masked, h + 1)
                    at = scored_at(h)
                    dve.tensor_tensor(scores[:, h, 0, :], at[:, 0:P], mg[:, 0, :], ALU.mult).then_inc(done, 1)
                    dve.scalar_tensor_tensor(scores[:, h, 1, :], at[:, P:S], beta_neg[:, c, h:h + 1], mg[:, 1, :],
                                             ALU.mult, ALU.mult).then_inc(done, 1)
        invert(prog, scores[:, :, 1, :], full, full_T, part, product)
        with prog.phase() as ph:
            carried, rhs_ready, u_made, u_copied, y_made, done = (
                ph.semaphore(n) for n in ("carried", "rhs_ready", "u_made", "u_copied", "y_made", "done"))

            @ph.block.tensor
            def _(pe):
                heads = [(h, slice(h % 2 * HD, h % 2 * HD + HD), slice(h * HD, (h + 1) * HD)) for h in range(NH8)]
                if c:
                    for x, bank in ((1, 0), (0, 3)):
                        for h, half, cols in heads:
                            last = pe.matmul(by_parity(psum, bank, h), qk[half, h // 2, c, x, :], state[half, h // 2, :],
                                             start=True, stop=True)
                        last.then_inc(carried, 1)
                    pe.wait_ge(rhs_ready, 2)
                for h, half, cols in heads:
                    last = pe.matmul(psum[:, 1, cols], full_T[:, h, :], rhs[:, h, :] if c else v_tok[:, c, cols],
                                     start=True, stop=True)
                last.then_inc(u_made, 1)
                pe.wait_ge(u_copied, 1)
                for h, half, cols in heads:
                    last = pe.matmul(psum[:, 2, cols], scores[:, h, 0, :], u[:, h, :], start=True, stop=True)
                last.then_inc(y_made, 1)
                if c == 0:
                    pe.wait_ge(u_copied, 2)
                    for h, half, cols in heads:
                        last = pe.matmul(psum[half, 3, h // 2 * HD:(h // 2 + 1) * HD], k_tok[:, c, cols], u2[:, h, :],
                                         start=True, stop=True)
                    last.then_inc(y_made, 1)

            @ph.block.vector
            def _(dve):
                if c:
                    dve.wait_ge(carried, 2)
                    dve.tensor_tensor(paired(rhs), both_parities(psum, 0), paired(per_head(grown[:, c, :])), ALU.mult).then_inc(rhs_ready, 1)
                    dve.wait_ge(rhs_ready, 1)
                    dve.tensor_tensor(rhs, heads_v(v_tok[:, c, :]), rhs, ALU.subtract).then_inc(rhs_ready, 1)
                    dve.tensor_tensor(paired(u2), both_parities(psum, 3), paired(per_head(grown[:, c, :])), ALU.mult).then_inc(rhs_ready, 1)
                dve.wait_ge(u_made, 1)
                dve.tensor_tensor(u, heads_v(psum[:, 1, :]), per_head(beta[:, c, :]), ALU.mult).then_inc(u_copied, 1)
                if c == 0:
                    dve.wait_ge(u_copied, 1)
                    dve.tensor_tensor(u2, u, per_head(left[:, c, :]), ALU.mult).then_inc(u_copied, 1)
                    dve.wait_ge(y_made, 1)
                    dve.tensor_copy(y[:, c, :], psum[:, 2, :]).then_inc(done, 1)
                    dve.wait_ge(y_made, 2)
                    dve.tensor_copy(state, psum[:, 3, 0:PAIRS * HD].rearrange("p (i d) -> p i d", i=PAIRS)).then_inc(done, 1)
                else:
                    dve.wait_ge(y_made, 1)
                    dve.wait_ge(rhs_ready, 3)
                    dve.tensor_tensor(heads_v(y[:, c, :]), heads_v(psum[:, 2, :]), u2, ALU.add).then_inc(done, 1)
    m = Free(prog, Arena(prog, at + 8 * S + 300), spare)
    sq, stat = m.take(TB, NH8, HD), m.take(TB, NH8)
    yh = y.rearrange("p b (h d) -> p b h d", h=NH8)
    head_norm(prog, yh, gain, 1.0 / HD, sq, stat)
    prog.solo("vector", lambda do: do(do.eng.tensor_tensor(y, y, gate_s, ALU.mult)))


def head_norm(prog, v, gain, inverse_width, squares, stat):
    nb, nh, n = v.shape[1:]

    def sums(do):
        dve = do.eng
        do(dve.tensor_tensor(squares, v, v, ALU.mult))
        do(dve.tensor_reduce(stat, squares, AX, ALU.add))
        do(dve.tensor_scalar(stat, stat, inverse_width, EPS, ALU.mult, ALU.add))

    prog.solo("vector", sums)
    prog.solo("scalar", lambda do: do(do.eng.activation(stat, stat, ACT.Sqrt)))

    def scales(do):
        do(do.eng.reciprocal(stat, stat))
        do(do.eng.tensor_tensor(v, v, spread(stat.unsqueeze(3), nb, nh, n), ALU.mult))
        for b in range(nb):
            do(do.eng.tensor_tensor(v[:, b], v[:, b], spread(gain.unsqueeze(1), nh, n), ALU.mult))

    prog.solo("vector", scales)


def mla_branch(prog, layer, z, o, at):
    NOPE, PE_W, QK = 64, 32, 96
    mem = Arena(prog, at)
    flat = lambda v: v.rearrange("p a b -> p (a b)")
    up = mem.take(2 * 768 + 1024)
    prog.load(up, prog.inp[f"mla_up{layer}"])
    w_q = up[:, 0:1536].rearrange("p (k n) -> p k n", k=2)
    w_kv = up[:, 1536:2560]
    gain_q, gain_k = mem.take(QK), mem.take(QK)
    prog.load_row(gain_q, f"mla_qk_norm_q_2{layer}")
    prog.load_row(gain_k, f"mla_qk_norm_k_2{layer}")
    q, k, kv = mem.take(TB, NH8, QK), mem.take(TB, NH8, QK), mem.take(TB, D)
    squares, stat = mem.take(TB, NH8, QK), mem.take(TB, NH8)
    cT, scale_q, scale_kv = mem.take(3, S), mem.take(TB), mem.take(TB)
    row_scales(prog, z[:, :, 0:256], 256, scale_q, kv[:, :, 0:256])
    row_scales(prog, z[:, :, 256:384], P, scale_kv, kv[:, :, 0:P])

    def scale_rows(do):
        for b in range(TB):
            do(do.eng.tensor_scalar(z[:, b, 0:256], z[:, b, 0:256], scale_q[:, b:b + 1], None, ALU.mult),
               do.eng.tensor_scalar(z[:, b, 256:384], z[:, b, 256:384], scale_kv[:, b:b + 1], None, ALU.mult))

    prog.solo("vector", scale_rows)
    first = prog.col_at[f"mla_q_norm_g_2{layer}"][0]
    transposes(prog, pair_sources(z[:, :, 0:384], 3), flat(cT), gains=prog.cols[:, first:first + 3])
    with prog.phase() as ph:
        q_made, kv_made, taken = ph.semaphore("q_made"), ph.semaphore("kv_made"), ph.semaphore("taken")

        @ph.block.tensor
        def _(pe):
            for b in range(TB):
                t = slice(b * P, (b + 1) * P)
                for n in range(2):
                    for i in range(2):
                        last = pe.matmul(prog.psum[:, 2 * b + n, 0:384], cT[:, i, t], w_q[:, i, n * 384:(n + 1) * 384],
                                         start=(i == 0), stop=(i == 1))
                last.then_inc(q_made, 1)
                for n in range(2):
                    last = pe.matmul(prog.psum[:, 4 + 2 * b + n, :], cT[:, 2, t], w_kv[:, n * BANK:(n + 1) * BANK],
                                     start=True, stop=True)
                last.then_inc(kv_made, 1)

        @ph.block.vector
        def _(dve):
            for b in range(TB):
                dve.wait_ge(q_made, b + 1)
                dve.tensor_copy(q[:, b].rearrange("p h d -> p (h d)").rearrange("p (n c) -> p n c", n=2),
                                prog.psum[:, 2 * b:2 * b + 2, 0:384]).then_inc(taken, 1)

        @ph.block.scalar
        def _(act):
            for b in range(TB):
                act.wait_ge(kv_made, b + 1)
                act.activation(kv[:, b, :].rearrange("p (n c) -> p n c", n=2), prog.psum[:, 4 + 2 * b:6 + 2 * b, :],
                               ACT.Copy).then_inc(taken, 1)

    def keys(do):
        for b in range(TB):
            do(do.eng.tensor_copy(k[:, b, :, 0:NOPE], kv[:, b, :].rearrange("p (h d) -> p h d", h=NH8)[:, :, 0:NOPE]),
               do.eng.tensor_copy(k[:, b, :, NOPE:QK], spread(z[:, b, 384:384 + PE_W].unsqueeze(1), NH8, PE_W)))

    prog.solo("vector", keys)
    head_norm(prog, q, gain_q, 1.0 / QK, squares, stat)
    head_norm(prog, k, gain_k, 1.0 / QK, squares, stat)
    work = squares.rearrange("p b h d -> p (b h d)")

    def rotations(do):
        for v in (q, k):
            rotate(do, prog, v[:, :, :, NOPE:QK], 12, 16, work)

    prog.solo("vector", rotations)
    qT, kT = mem.take(NH8, S), mem.take(NH8, S)
    for v, t in ((q, qT), (k, kT)):
        transposes(prog, [v[:, b, h, :] for h in range(NH8) for b in range(TB)], flat(t), width=QK)
    heads = [(qT[0:QK, h, :], kT[0:QK, h, :], lambda b, h=h: kv[:, b, h * P + NOPE:(h + 1) * P],
              lambda b, h=h: o[:, b, BANK + h * HD:BANK + (h + 1) * HD], None, False) for h in range(NH8)]
    attention(prog, causal_jobs(prog, heads, QK ** -0.5), Arena(prog, mem.at))


def project_features(prog, weights, widths, xT, zT):
    tiles = [(c, f) for c, n in enumerate(widths) for f in range(n // P)]
    with prog.phase() as ph:
        tile_full = ph.semaphore("tile_full")
        emptied = [ph.semaphore("emptied_by_scalar"), ph.semaphore("emptied_by_vector")]

        @ph.block.sync
        def _(sp):
            weights.rest(sp, tile_full, 4)

        @ph.block.tensor
        def _(pe):
            for i, (c, f) in enumerate(tiles):
                if f == 0:
                    weights.wait(pe, c)
                    w = weights.buffer(c).rearrange("p (k n) -> p k n", k=KT)
                b = i // 2
                if i % 2 == 0 and b >= 8:
                    pe.wait_ge(emptied[b % 2], (b - 8) // 2 + 1)
                for k in range(KT):
                    last = pe.matmul(prog.psum[:, b % 8, i % 2 * S:(i % 2 + 1) * S], w[:, k, f * P:(f + 1) * P],
                                     xT[:, k, :], start=(k == 0), stop=(k == KT - 1))
                last.then_inc(tile_full, 1)

        def empty(eng, which, copy):
            for b in range(len(tiles) // 2):
                if b % 2 == which:
                    eng.wait_ge(tile_full, 2 * b + 2)
                    copy(zT[:, 2 * b:2 * b + 2, :].rearrange("p i t -> p (i t)"), prog.psum[:, b % 8, :])\
                        .then_inc(emptied[which], 1)

        @ph.block.scalar
        def _(act):
            empty(act, 0, lambda o, i: act.activation(o, i, ACT.Copy))

        @ph.block.vector
        def _(dve):
            empty(dve, 1, lambda o, i: dve.tensor_copy(o, i))


def merge(prog, weights, oT, merged):
    mem_gate = Arena(prog, merged[1])
    gates, sums = mem_gate.take(2, BANK), mem_gate.take(BANK)
    merged = merged[0]
    steps = [(j, x, b) for j in range(2) for x in range(3) for b in range(TB)]
    added_before = np.cumsum([0] + [x > 0 for j, x, b in steps]).tolist()
    with prog.phase() as ph:
        gate_sum, branch_sum, squashed, weighted, added = (
            ph.semaphore(n) for n in ("gate_sum", "branch_sum", "squashed", "weighted", "added"))

        @ph.block.sync
        def _(sp):
            for i in range(weights.ahead, len(weights.pieces)):
                n = i - weights.slots
                sp.wait_ge(gate_sum if n % 2 == 0 else branch_sum, TB * (n // 2 + 1))
                weights.start(sp, i)

        @ph.block.tensor
        def _(pe):
            for n, (j, x, b) in enumerate(steps):
                piece, t = 2 * (3 * j + x), slice(b * P, (b + 1) * P)
                if n >= 4:
                    pe.wait_ge(weighted, n - 3)
                weights.wait(pe, piece)
                w = weights.buffer(piece).rearrange("p (k n) -> p k n", k=KT)
                for k in range(KT):
                    last = pe.matmul(prog.psum[:, 2 * (n % 4), :], prog.xT[:, k, t], w[:, k, :], start=(k == 0), stop=(k == KT - 1))
                last.then_inc(gate_sum, 1)
                weights.wait(pe, piece + 1)
                w = weights.buffer(piece + 1).rearrange("p (k n) -> p k n", k=4)
                for k in range(4):
                    last = pe.matmul(prog.psum[:, 2 * (n % 4) + 1, :], oT[:, 4 * x + k, t], w[:, k, :], start=(k == 0), stop=(k == 3))
                last.then_inc(branch_sum, 1)

        @ph.block.scalar
        def _(act):
            for n in range(len(steps)):
                act.wait_ge(gate_sum, n + 1)
                if n >= 2:
                    act.wait_ge(weighted, n - 1)
                act.activation(gates[:, n % 2, :], prog.psum[:, 2 * (n % 4), :], ACT.Sigmoid).then_inc(squashed, 1)

        @ph.block.vector
        def _(dve):
            for n, (j, x, b) in enumerate(steps):
                dve.wait_ge(squashed, n + 1)
                dve.wait_ge(branch_sum, n + 1)
                at = merged[:, b, j * BANK:(j + 1) * BANK]
                ps = prog.psum[:, 2 * (n % 4) + 1, :]
                if x == 0:
                    dve.tensor_tensor(at, gates[:, n % 2, :], ps, ALU.mult).then_inc(weighted, 1)
                else:
                    if added_before[n]:
                        dve.wait_ge(added, added_before[n])
                    dve.tensor_tensor(sums, gates[:, n % 2, :], ps, ALU.mult).then_inc(weighted, 1)
                    dve.wait_ge(weighted, n + 1)
                    dve.tensor_tensor(at, at, sums, ALU.add).then_inc(added, 1)


SHARES, PICKED = 7, 18
MAX_JOBS = 11


def mixture(prog, stream, xn, gain, at):
    NE, PIECES, SLOTS, NB = 8, 28, 4, 16
    PIECE = 3 * D
    psum = prog.psum
    mem = Arena(prog, at)
    router = mem.take(KT, NE)
    prog.load(router.rearrange("p k e -> p (k e)"), prog.inp["router"])
    top, top_i, top_f = mem.take(TB, 8), mem.take(TB, 8).bitcast(U32), mem.take(TB, 8)
    logits, w, picked, share = mem.take(TB, NE), mem.take(TB, NE), mem.take(TB, NE), mem.take(TB, 2)
    taken, place = mem.take(TB, NE), mem.take(TB, NE)
    exists, order = mem.take(NB), mem.take(NB)
    is_job, job_expert = mem.take(MAX_JOBS, NB), mem.take(MAX_JOBS, NE)
    job_work, first_place = mem.take(MAX_JOBS, NB), mem.take(MAX_JOBS)
    table_f, table = mem.take(MAX_JOBS + 1), mem.take(MAX_JOBS + 1).bitcast(I32)
    job_place, job_weight = mem.take(TB, MAX_JOBS), mem.take(TB, MAX_JOBS)

    with prog.phase() as ph:
        made, shared, done = ph.semaphore("made"), ph.semaphore("shared"), ph.semaphore("done")
        ranked = ph.semaphore("ranked")

        @ph.block.tensor
        def _(pe):
            prog.wait_small(pe)
            for b in range(TB):
                for k in range(KT):
                    last = pe.matmul(psum[:, b, 0:NE], prog.xT[:, k, b * P:(b + 1) * P], router[:, k, :],
                                     start=(k == 0), stop=(k == KT - 1))
            last.then_inc(made, 1)
            pe.wait_ge(done, PICKED)
            pe.matmul(psum[:, 2, 0:NE], prog.const("strict"), taken[:, 0, :], start=True, stop=True)
            pe.matmul(psum[:, 3, 0:NE], prog.const("ones"), taken[:, 0, :], start=True, stop=False)
            pe.matmul(psum[:, 3, 0:NE], prog.const("strict"), taken[:, 1, :], start=False, stop=True)
            pe.matmul(psum[:, 4, 0:NE], prog.const("ones"), taken[:, 0, :], start=True, stop=False)
            pe.matmul(psum[:, 4, 0:NE], prog.const("ones"), taken[:, 1, :], start=False, stop=True).then_inc(ranked, 1)

        @ph.block.scalar
        def _(act):
            act.wait_ge(done, SHARES)
            act.activation(share[:, :, 0], share[:, :, 1], ACT.Sigmoid, scale=-1.0).then_inc(shared, 1)
            act.wait_ge(shared, 1)
            act.activation(share[:, :, 1], share[:, :, 1], ACT.Sigmoid).then_inc(shared, 1)

        @ph.block.vector
        def _(dve):
            do = Steps(dve, done)
            dve.wait_ge(made, 1)
            for b in range(TB):
                do(dve.tensor_copy(logits[:, b, :], psum[:, b, 0:NE]))
                do(dve.max(top[:, b, :], logits[:, b, :]))
                do(dve.max_index(top_i[:, b, :], top[:, b, :], logits[:, b, :]))
            do(dve.tensor_tensor(share[:, :, 1], top[:, :, 1], top[:, :, 0], ALU.subtract))
            assert do.n == SHARES
            do(dve.tensor_copy(top_f, top_i))
            dve.wait_ge(shared, 2)
            numbers = prog.const("iota")[:, 0:NE]
            for b in range(TB):
                do(dve.tensor_scalar(taken[:, b, :], numbers, top_f[:, b, 0:1], None, ALU.is_equal))
                do(dve.tensor_scalar(w[:, b, :], taken[:, b, :], share[:, b, 0:1], None, ALU.mult))
                do(dve.tensor_scalar(picked[:, b, :], numbers, top_f[:, b, 1:2], None, ALU.is_equal))
                do(dve.scalar_tensor_tensor(w[:, b, :], picked[:, b, :], share[:, b, 1:2], w[:, b, :], ALU.mult, ALU.add),
                   dve.tensor_tensor(taken[:, b, :], taken[:, b, :], picked[:, b, :], ALU.add))
            assert do.n == PICKED
            dve.wait_ge(ranked, 1)
            ex = exists.rearrange("p (e i) -> p e i", i=2)
            do(dve.tensor_scalar(ex[:, :, 0], psum[:, 4, 0:NE], 0.0, None, ALU.is_gt),
               dve.tensor_scalar(ex[:, :, 1], psum[:, 4, 0:NE], float(P), None, ALU.is_gt),
               dve.tensor_copy(place, psum[:, 2:4, 0:NE]))
            do(dve.tensor_tensor_scan(order, prog.const("ones")[:, 0:NB], exists, 0.0, ALU.mult, ALU.add))
            do(dve.tensor_copy(table_f[:, MAX_JOBS:MAX_JOBS + 1], order[:, NB - 1:NB]))
            do(dve.tensor_tensor(order, order, exists, ALU.mult))
            do(dve.tensor_tensor(is_job, spread(prog.const("iota")[:, 1:MAX_JOBS + 1].unsqueeze(2), MAX_JOBS, NB),
                                 spread(order.unsqueeze(1), MAX_JOBS, NB), ALU.is_equal))
            jb = is_job.rearrange("p k (e i) -> p k e i", i=2)
            do(dve.tensor_tensor(job_expert, jb[:, :, :, 0], jb[:, :, :, 1], ALU.add))
            do(dve.tensor_reduce(first_place, jb[:, :, :, 1], AX, ALU.add))
            do(dve.tensor_scalar(first_place, first_place, float(P), None, ALU.mult),
               dve.tensor_tensor(job_work[:, :, 0:NE], job_expert, spread(numbers.unsqueeze(1), MAX_JOBS, NE), ALU.mult))
            do(dve.tensor_reduce(table_f[:, 0:MAX_JOBS], job_work[:, :, 0:NE], AX, ALU.add))
            do(dve.tensor_copy(table, table_f))
            do(dve.tensor_scalar(taken, taken, -1024.0, 1024.0, ALU.mult, ALU.add))
            do(dve.tensor_tensor(place, place, taken, ALU.add))
            for b in range(TB):
                for value, out in ((place, job_place), (w, job_weight)):
                    do(dve.tensor_tensor(job_work[:, :, 0:NE], job_expert, spread(value[:, b, :].unsqueeze(1), MAX_JOBS, NE), ALU.mult))
                    do(dve.tensor_reduce(out[:, b, :], job_work[:, :, 0:NE], AX, ALU.add))
                do(dve.tensor_tensor(job_place[:, b, :], job_place[:, b, :], first_place, ALU.subtract))

    pick, pick_w, turned_w = mem.take(TB, P), mem.take(TB, P), mem.take(TB, P)
    xg, hidden, silu, rows = mem.take(KT, P), mem.take(2, P), mem.take(2, P), mem.take(D)
    slot = lambda s: prog.ring[:, s * PIECE:(s + 1) * PIECE]
    base = list(prog.n_slot)
    with prog.phase() as ph:
        (slot_free, picks_ready, turned, turned_copied, gathered, gathered_copied, tile_ready, silu_ready,
         hidden_ready, job_copied, job_added) = (ph.semaphore(n) for n in (
             "slot_free", "picks_ready", "turned", "turned_copied", "gathered", "gathered_copied", "tile_ready",
             "silu_ready", "hidden_ready", "job_copied", "job_added"))
        jobs_of = lambda eng: eng.value_load(table[0:1, MAX_JOBS:MAX_JOBS + 1], min_val=1, max_val=MAX_JOBS)

        @ph.block.sync
        def _(sp):
            n_jobs = jobs_of(sp)
            with sp.Fori(0, n_jobs) as k:
                expert = sp.value_load(table[0:1, bass.ds(k, 1)], min_val=0, max_val=NE - 1)
                with sp.Fori(0, PIECES // SLOTS) as r:
                    for s in range(SLOTS):
                        sp.wait_ge(slot_free, k * PIECES + r * SLOTS + s + 1)
                        sp.dma_start(slot(s), stream[bass.ds(expert * PIECES + r * SLOTS + s, 1), :, :]
                                     .rearrange("g p c -> p (g c)")).then_inc(prog.slot_loaded[s], 16)

        @ph.block.tensor
        def _(pe):
            n_jobs = jobs_of(pe)
            zeros = prog.const("zero")[:, 0:64].bitcast(BF16)
            for b in range(4):
                pe.matmul(psum[:, 4 + b, :], zeros, zeros_wide(prog), start=True, stop=False,
                          skip_group_check=True).then_inc(slot_free, 1)
            with pe.Fori(0, n_jobs) as k:
                pe.wait_ge(picks_ready, k + 1)
                for b in range(TB):
                    last = pe.transpose(psum[:, 2, b * P:(b + 1) * P], pick_w[:, b, :], prog.ident)
                last.then_inc(turned, 1)
                for i in range(KT):
                    for b in range(TB):
                        last = pe.matmul(psum[:, i // 4, i % 4 * P:(i % 4 + 1) * P], xn[:, b, i * P:(i + 1) * P],
                                         pick[:, b, :], start=(b == 0), stop=(b == TB - 1))
                last.then_inc(gathered, 1)
                pe.wait_ge(turned_copied, k + 1)
                for n in range(2):
                    pe.matmul(psum[:, 2 + n, :], zeros, zeros_wide(prog), start=True, stop=False, skip_group_check=True)
                pe.wait_ge(gathered_copied, 2 * k + 2)

                def gate_up(r, s):
                    pe.wait_ge(prog.slot_loaded[s], k * (16 * PIECES // SLOTS) + r * 16 + 16 * (base[s] + 1))
                    m = slot(s).rearrange("p (m k f) -> p m k f", m=3, k=KT)
                    for x in range(2):
                        for i in range(KT):
                            last = pe.matmul(psum[:, s % 2, x * P:(x + 1) * P], m[:, x, i, :], xg[:, i, :],
                                             start=(i == 0), stop=(i == KT - 1))
                    last.then_inc(tile_ready, 1)

                def down(r, s):
                    pe.wait_ge(hidden_ready, k * PIECES + r * SLOTS + s + 1)
                    for n in range(2):
                        last = pe.matmul(psum[:, 2 + n, :], hidden[:, s % 2, :],
                                         slot(s)[:, 2 * D + n * BANK:2 * D + (n + 1) * BANK], start=False, stop=False,
                                         skip_group_check=True)
                    last.then_inc(slot_free, 1)
                    return last

                gate_up(0, 0)
                with pe.Fori(0, PIECES // SLOTS - 1) as r:
                    for s in range(SLOTS):
                        gate_up(r + (s + 1) // SLOTS, (s + 1) % SLOTS)
                        down(r, s)
                last_round = PIECES // SLOTS - 1
                for s in range(SLOTS - 1):
                    gate_up(last_round, s + 1)
                    down(last_round, s)
                down(last_round, SLOTS - 1)
                pe.wait_ge(job_copied, 2 * k + 2)
                for b in range(TB):
                    for n in range(2):
                        last = pe.matmul(psum[:, 4 + 2 * b + n, :], turned_w[:, b, :], rows[:, n * BANK:(n + 1) * BANK],
                                         start=False, stop=False, skip_group_check=True)
                last.then_inc(job_added, 1)

        @ph.block.scalar
        def _(act):
            n_jobs = jobs_of(act)
            with act.Fori(0, n_jobs * (PIECES // SLOTS)) as n:
                for t in range(SLOTS):
                    act.wait_ge(tile_ready, n * SLOTS + t + 1)
                    act.activation(silu[:, t % 2, :], psum[:, t % 2, 0:P], ACT.Silu).then_inc(silu_ready, 1)

        @ph.block.vector
        def _(dve):
            n_jobs = jobs_of(dve)
            with dve.Fori(0, n_jobs) as k:
                iota = prog.const("iota")
                for b in range(TB):
                    at = job_place[:, b, bass.ds(k, 1)]
                    dve.tensor_scalar(pick[:, b, :], iota, at, None, ALU.is_equal)
                    last = dve.tensor_scalar(pick_w[:, b, :], iota, at, job_weight[:, b, bass.ds(k, 1)], ALU.is_equal, ALU.mult)
                last.then_inc(picks_ready, 1)
                dve.wait_ge(turned, k + 1)
                dve.tensor_copy(turned_w.rearrange("p b t -> p (b t)"), psum[:, 2, 0:S]).then_inc(turned_copied, 1)
                dve.wait_ge(gathered, k + 1)
                for n in range(2):
                    dve.tensor_tensor(xg[:, 4 * n:4 * n + 4, :], psum[:, n, :].rearrange("p (i t) -> p i t", i=4),
                                      spread(gain[:, 4 * n:4 * n + 4].unsqueeze(2), 4, P), ALU.mult).then_inc(gathered_copied, 1)
                with dve.Fori(0, PIECES // 2) as n:
                    for t in range(2):
                        dve.wait_ge(silu_ready, k * PIECES + n * 2 + t + 1)
                        dve.tensor_tensor(hidden[:, t, :], silu[:, t, :], psum[:, t, P:2 * P], ALU.mult).then_inc(hidden_ready, 1)
                dve.wait_ge(slot_free, (k + 1) * PIECES + SLOTS)
                for n in range(2):
                    dve.tensor_copy(rows[:, n * BANK:(n + 1) * BANK], psum[:, 2 + n, :]).then_inc(job_copied, 1)
                dve.wait_ge(job_added, k + 1)
            for b in range(TB):
                for n in range(2):
                    out = prog.x[:, b, n * BANK:(n + 1) * BANK]
                    dve.tensor_tensor(out, psum[:, 4 + 2 * b + n, :], out, ALU.add)


def embedding(prog, layer, weights):
    mem = Arena(prog)
    flat = lambda v: v.rearrange("p a b -> p (a b)")
    pT, proj, gain = mem.take(2, S), mem.take(2, D), mem.take(D)
    e, work, scale, gates = mem.take(TB, D), mem.take(TB, D), mem.take(TB), mem.take(TB, D)
    prog.load(flat(pT), prog.inp[f"pT{layer}"])
    prog.load(flat(proj), prog.inp[f"ple_proj{layer}"])
    prog.load_row(gain, f"ple_norm_g_2{layer}")
    with prog.phase() as ph:
        made, taken = ph.semaphore("made"), ph.semaphore("taken")

        @ph.block.tensor
        def _(pe):
            prog.wait_small(pe)
            for b in range(TB):
                for n in range(2):
                    for i in range(2):
                        last = pe.matmul(prog.psum[:, 2 * b + n, :], pT[:, i, b * P:(b + 1) * P],
                                         proj[:, i, n * BANK:(n + 1) * BANK], start=(i == 0), stop=(i == 1))
                last.then_inc(made, 1)

        @ph.block.scalar
        def _(act):
            for b in range(TB):
                act.wait_ge(made, b + 1)
                act.activation(e[:, b, :].rearrange("p (n c) -> p n c", n=2), prog.psum[:, 2 * b:2 * b + 2, :], ACT.Copy)\
                   .then_inc(taken, 1)
    row_scales(prog, e, D, scale, work)

    def scale_rows(do):
        for b in range(TB):
            do(do.eng.scalar_tensor_tensor(e[:, b, :], e[:, b, :], scale[:, b:b + 1], gain, ALU.mult, ALU.mult))

    prog.solo("vector", scale_rows)
    transposes(prog, [prog.x[:, b, k * P:(k + 1) * P] for k in range(KT) for b in range(TB)], prog.xT_sb[:])
    with prog.phase() as ph:
        bank_full, squashed, weighted, done = (ph.semaphore(n) for n in ("bank_full", "squashed", "weighted", "done"))
        order = [(c, b) for c in range(2) for b in range(TB)]

        @ph.block.tensor
        def _(pe):
            for c, b in order:
                weights.wait(pe, c)
                w = weights.buffer(c).rearrange("p (k n) -> p k n", k=KT)
                for k in range(KT):
                    last = pe.matmul(prog.psum[:, 2 * c + b, :], prog.xT[:, k, b * P:(b + 1) * P], w[:, k, :],
                                     start=(k == 0), stop=(k == KT - 1))
                last.then_inc(bank_full, 1)

        @ph.block.scalar
        def _(act):
            for n, (c, b) in enumerate(order):
                act.wait_ge(bank_full, n + 1)
                act.activation(gates[:, b, c * BANK:(c + 1) * BANK], prog.psum[:, 2 * c + b, :], ACT.Sigmoid).then_inc(squashed, 1)

        @ph.block.vector
        def _(dve):
            for n, (c, b) in enumerate(order):
                cols = slice(c * BANK, (c + 1) * BANK)
                dve.wait_ge(squashed, n + 1)
                dve.tensor_tensor(e[:, b, cols], e[:, b, cols], gates[:, b, cols], ALU.mult).then_inc(weighted, 1)
                dve.wait_ge(weighted, n + 1)
                dve.tensor_tensor(prog.x[:, b, cols], prog.x[:, b, cols], e[:, b, cols], ALU.add).then_inc(done, 1)


def second_memory(prog):
    mem = Arena(prog, prog.arena_size - PAIRS * S)
    v_first = mem.take(PAIRS, S)
    prog.arena_size -= PAIRS * S
    mem = Arena(prog)
    z_tok, o, zT = mem.take(TB, 944), mem.take(TB, 3 * BANK), mem.take(26, S)
    return zT, o, v_first, z_tok, mem.at


def mla_at(prog):
    return TB * 944 + TB * 3 * BANK


def second_weights(prog, layer):
    feat = chunk_weights(prog, prog.inp[f"feat_w{layer}"], FEAT_CHUNKS)
    tok = chunk_weights(prog, prog.inp[f"tok_w{layer}"], TOK_CHUNKS)
    flat, pieces, at = prog.inp[f"merge_w{layer}"], [], 0
    for i in range(12):
        n = P * (KT if i % 2 == 0 else 4) * BANK
        pieces.append(flat[at:at + n].rearrange("(p c) -> p c", p=P))
        at += n
    return feat, tok, Weights(prog, pieces, 4, KT * BANK)


def build(nc, inp, tables, out):
    prog = Program(nc, inp, tables)
    with prog.ctx:
        prog.load(prog.consts[:], inp["consts"])
        prog.load(prog.cols[:], inp["cols"])
        prog.load(prog.x_sb[:], inp["x"])
        ffn = [group_stream(prog, inp["ffn_w"], 11 * i, 11) for i in range(5)]
        rope_tables(prog)
        ev_in, ev_out = chunk_weights(prog, inp["ev_in_w"], EVEN_CHUNKS), chunk_weights(prog, inp["ev_out_w"], OUT_CHUNKS)
        od_in, od_out = chunk_weights(prog, inp["od_in_w"], ODD_CHUNKS), chunk_weights(prog, inp["od_out_w"], OUT_CHUNKS)
        def ff(k, i, gain, factor=0.5):
            ffn[i].prefetch()
            norm_transposed(prog, prog.col(gain))
            feed_forward(prog, ffn[i], 11, factor)
        ff(1, 0, "ffn1_norm0")
        ev_in.prefetch()
        norm_transposed(prog, prog.col("mix_norm0"))
        even_mixer(prog, ev_in, ev_out)
        ff(3, 1, "ffn2_norm0")
        ff(4, 2, "ffn1_norm1")
        od_in.prefetch()
        norm_transposed(prog, prog.col("mix_norm1"))
        odd_mixer(prog, od_in, od_out)
        ff(6, 3, "ffn2_norm1")
        final_norm(prog)
        zT, o, v_first, z_tok, base = second_memory(prog)
        for i in range(2):
            feat, tok, mer = second_weights(prog, i)
            out_w = chunk_weights(prog, inp[f"out_w{i}"], OUT_CHUNKS)
            ple_w = chunk_weights(prog, inp[f"ple_gate{i}"], OUT_CHUNKS)
            feat.prefetch()
            norm_transposed(prog, prog.col(f"norm_mix_g_2{i}"), base)
            project_features(prog, feat, FEAT_CHUNKS, prog.xT, zT)
            tok.prefetch()
            project(prog, tok, TOK_CHUNKS, prog.xT, copy_to(z_tok))
            rwkv_branch(prog, i, zT, o, v_first, base)
            gdn_branch(prog, i, zT[:, 14:26], z_tok[:, :, 416:432], z_tok[:, :, 432:944], o, base)
            mer.prefetch()
            mla_branch(prog, i, z_tok, o, mla_at(prog))
            mem = Arena(prog, mla_at(prog))
            oT = mem.take(12, S)
            transposes(prog, [o[:, b, k * P:(k + 1) * P] for k in range(12) for b in range(TB)], oT.rearrange("p a b -> p (a b)"))
            merged, mT = mem.take(TB, D), mem.take(KT, S)
            merge(prog, mer, oT, (merged, mem.at))
            out_w.prefetch()
            transposes(prog, [merged[:, b, k * P:(k + 1) * P] for k in range(KT) for b in range(TB)], mT.rearrange("p a b -> p (a b)"))
            add_projection(prog, out_w, mT)
            if i == 0:
                ffn[4].prefetch()
                norm_transposed(prog, prog.col("norm_ffn_g_20"), base)
                feed_forward(prog, ffn[4], 11)
            else:
                xn = Arena(prog).take(TB, D)
                norm_transposed(prog, prog.col("norm_ffn_g_21"))
                mixture(prog, inp["moe_w"], xn, prog.col("norm_ffn_g_21"), TB * D + TB)
            ple_w.prefetch()
            embedding(prog, i, ple_w)
        stored = prog.ctx.enter_context(nc.semaphore("stored"))
        with prog.phase() as ph:
            @ph.block.sync
            def _(sp):
                sp.dma_start(out, prog.x_sb[:]).then_inc(stored, 16)
                sp.wait_ge(stored, 16)
        prog.before.ctx.close()


def kernel(**inputs):
    import concourse.bacc as bacc
    from concourse.bass_utils import run_bass_kernel_spmd

    nc = bacc.Bacc("TRN2", target_bir_lowering=False, num_devices=1)
    arrays = {f"in_{k}": v for k, v in lay_out(inputs).items()}
    aps = {k[3:]: nc.dram_tensor(k, v.shape, mybir.dt.from_np(v.dtype), kind="ExternalInput").ap()
           for k, v in arrays.items()}
    out = nc.dram_tensor("out", (P, TB * D), F32, kind="ExternalOutput").ap()
    tables = constant_table()[1], column_table(inputs)[1], row_table(inputs)[1]
    build(nc, aps, tables, out)
    got = run_bass_kernel_spmd(nc, [arrays], core_ids=[0]).results[0]["out"]
    return got.reshape(P, TB, D).transpose(1, 0, 2).reshape(1, S, D)
```
